# Optimizing a Trainium2 kernel written in Bass

```python
import jax, jax.numpy as jnp
from jax import lax
import numpy as np

D_MODEL = 1024
BATCH = 1
SEQ = 1024
DEPTH = 1

CHUNK = 64
LEFT_CHUNKS = 8
BAND = (LEFT_CHUNKS + 1) * CHUNK
D_MIX = D_MODEL
D_ATTN = D_MIX // 2
D_CONV = D_MIX - D_ATTN
HEAD_DIM = 64
N_HEADS = D_ATTN // HEAD_DIM
CONV_GROUPS = 8
CONV_WIDTH = 3
MAX_REL = 128
N_REL = 2 * MAX_REL + 1
D_FF = 2816
N_SUB = 3
FFN_RES = 0.5
EPS = 1e-6
NEG_INF = -1e30

kernel_name = "hybrid_chunked_attn_shortconv_macaron_adaln"

def rms_norm(x, g):
    xf = x.astype(jnp.float32)
    y = xf * lax.rsqrt(jnp.mean(xf * xf, axis=-1, keepdims=True) + EPS)
    return (y * g.astype(jnp.float32)).astype(x.dtype)

def adaln_pre(x, g, shift, scale):
    return rms_norm(x, g) * (1.0 + scale[:, None, :]) + shift[:, None, :]

def swiglu(h, w_gu, w_down):
    gu = h @ w_gu
    g, u = jnp.split(gu, 2, axis=-1)
    return (jax.nn.silu(g) * u) @ w_down

def chunked_rel_attention(q, k, v, rel_bias):
    B, S, H, Dh = q.shape
    nc = S // CHUNK
    pad = LEFT_CHUNKS * CHUNK
    k_pad = jnp.pad(k, ((0, 0), (pad, 0), (0, 0), (0, 0)))
    v_pad = jnp.pad(v, ((0, 0), (pad, 0), (0, 0), (0, 0)))
    q_chunks = q.reshape(B, nc, CHUNK, H, Dh).transpose(1, 0, 2, 3, 4)
    a = jnp.arange(CHUNK)[:, None]
    j = jnp.arange(BAND)[None, :]
    rel_idx = jnp.clip(j - pad - a, -MAX_REL, MAX_REL) + MAX_REL
    bias = rel_bias[:, rel_idx].astype(jnp.float32)
    sm_scale = HEAD_DIM ** -0.5

    def one_chunk(args):
        i, qc = args
        start = i * CHUNK
        kb = lax.dynamic_slice_in_dim(k_pad, start, BAND, axis=1)
        vb = lax.dynamic_slice_in_dim(v_pad, start, BAND, axis=1)
        s = jnp.einsum('bqhd,bkhd->bhqk', qc, kb,
                       preferred_element_type=jnp.float32) * sm_scale + bias
        key_pos = start - pad + jnp.arange(BAND)
        s = jnp.where((key_pos >= 0)[None, None, None, :], s, NEG_INF)
        p = jax.nn.softmax(s, axis=-1)
        return jnp.einsum('bhqk,bkhd->bqhd', p.astype(vb.dtype), vb)

    out = lax.map(one_chunk, (jnp.arange(nc), q_chunks))
    return out.transpose(1, 0, 2, 3, 4).reshape(B, S, H, Dh)

def causal_depthwise_conv(u, w_conv, b_conv):
    ch = u.shape[-1]
    y = lax.conv_general_dilated(
        u, w_conv[:, None, :].astype(u.dtype), window_strides=(1,),
        padding=[(CONV_WIDTH - 1, 0)], dimension_numbers=('NWC', 'WIO', 'NWC'),
        feature_group_count=ch)
    return y + b_conv

def hybrid_mixer(h, w_in, q_norm_g, k_norm_g, rel_bias, w_conv, b_conv,
                 g_attn_out, g_conv_out, w_out):
    B, S, _ = h.shape
    proj = h @ w_in
    q, k, v, xc, gate_b, gate_c = jnp.split(
        proj, [D_ATTN, 2 * D_ATTN, 3 * D_ATTN, 3 * D_ATTN + D_CONV,
               3 * D_ATTN + 2 * D_CONV], axis=-1)
    q = rms_norm(q.reshape(B, S, N_HEADS, HEAD_DIM), q_norm_g)
    k = rms_norm(k.reshape(B, S, N_HEADS, HEAD_DIM), k_norm_g)
    v = v.reshape(B, S, N_HEADS, HEAD_DIM)
    y_attn = chunked_rel_attention(q, k, v, rel_bias).reshape(B, S, D_ATTN)
    y_conv = gate_b * causal_depthwise_conv(gate_c * xc, w_conv, b_conv)
    y = jnp.concatenate([rms_norm(y_attn, g_attn_out), rms_norm(y_conv, g_conv_out)], axis=-1)
    return y @ w_out

def setup_inputs(seed: int = 0) -> dict:
    key = jax.random.key(seed)
    ks = jax.random.split(key, 24)
    f32 = jnp.float32
    D, L = D_MODEL, DEPTH
    nrm = lambda k, shape, s: jax.random.normal(k, shape, f32) * s
    return {
        "x": nrm(ks[0], (BATCH, SEQ, D), 1.0),
        "c": nrm(ks[1], (BATCH, D), 1.0),
        "w_ada": nrm(ks[2], (L, D, N_SUB * 3 * D), 0.1 * D ** -0.5),
        "b_ada": nrm(ks[3], (L, N_SUB * 3 * D), 0.01),
        "g_norm": 1.0 + nrm(ks[4], (L, N_SUB, D), 0.02),
        "w_ffn1_in": nrm(ks[5], (L, D, 2 * D_FF), D ** -0.5),
        "w_ffn1_out": nrm(ks[6], (L, D_FF, D), D_FF ** -0.5),
        "w_in": nrm(ks[7], (L, D, 3 * D_ATTN + 3 * D_CONV), D ** -0.5),
        "q_norm_g": 1.0 + nrm(ks[8], (L, HEAD_DIM), 0.02),
        "k_norm_g": 1.0 + nrm(ks[9], (L, HEAD_DIM), 0.02),
        "rel_bias": nrm(ks[10], (L, N_HEADS, N_REL), 0.2),
        "w_conv": nrm(ks[11], (L, CONV_WIDTH, D_CONV), CONV_WIDTH ** -0.5),
        "b_conv": nrm(ks[12], (L, D_CONV), 0.01),
        "g_attn_out": 1.0 + nrm(ks[13], (L, D_ATTN), 0.02),
        "g_conv_out": 1.0 + nrm(ks[14], (L, D_CONV), 0.02),
        "w_out": nrm(ks[15], (L, D_MIX, D), D_MIX ** -0.5),
        "w_ffn2_in": nrm(ks[16], (L, D, 2 * D_FF), D ** -0.5),
        "w_ffn2_out": nrm(ks[17], (L, D_FF, D), D_FF ** -0.5),
        "g_final": 1.0 + nrm(ks[18], (L, D), 0.02),
    }

def reference(x, c, w_ada, b_ada, g_norm, w_ffn1_in, w_ffn1_out, w_in, q_norm_g,
              k_norm_g, rel_bias, w_conv, b_conv, g_attn_out, g_conv_out, w_out,
              w_ffn2_in, w_ffn2_out, g_final):
    B = x.shape[0]
    for l in range(DEPTH):
        mod = (jax.nn.silu(c) @ w_ada[l] + b_ada[l]).reshape(B, N_SUB, 3, D_MODEL)
        shift, scale, gate = mod[:, :, 0], mod[:, :, 1], mod[:, :, 2]
        h = adaln_pre(x, g_norm[l, 0], shift[:, 0], scale[:, 0])
        x = x + FFN_RES * (1.0 + gate[:, 0])[:, None, :] * swiglu(h, w_ffn1_in[l], w_ffn1_out[l])
        h = adaln_pre(x, g_norm[l, 1], shift[:, 1], scale[:, 1])
        y = hybrid_mixer(h, w_in[l], q_norm_g[l], k_norm_g[l], rel_bias[l], w_conv[l],
                         b_conv[l], g_attn_out[l], g_conv_out[l], w_out[l])
        x = x + (1.0 + gate[:, 1])[:, None, :] * y
        h = adaln_pre(x, g_norm[l, 2], shift[:, 2], scale[:, 2])
        x = x + FFN_RES * (1.0 + gate[:, 2])[:, None, :] * swiglu(h, w_ffn2_in[l], w_ffn2_out[l])
        x = rms_norm(x, g_final[l])
    return x


_drawn_inputs = setup_inputs


def setup_inputs(seed=0):
    import zlib

    import numpy as np

    out = dict(_drawn_inputs(seed))
    spreads = {}
    factors = {'q_norm_g': 7.396,
     'k_norm_g': 6.485,
     'b_conv': 8.0,
     'g_attn_out': 105.656,
     'g_conv_out': 117.761,
     'g_final': 24.434,
     'rel_bias': 3.398,
     'w_ffn2_in': 4.925,
     'w_ffn2_out': 4.928}
    for name, (base, spread) in spreads.items():
        noise = np.random.default_rng([zlib.crc32(name.encode()), seed]).standard_normal(out[name].shape)
        drawn = base * np.exp(spread * noise) if base else spread * noise
        out[name] = __import__('jax').numpy.asarray(drawn.astype(out[name].dtype))
    for name, factor in factors.items():
        out[name] = (out[name] * factor).astype(out[name].dtype)
    return out
```

```python
from contextlib import ExitStack

import concourse.bass as bass
from concourse import mybir

F32 = mybir.dt.float32
F32R = mybir.dt.float32r
ALU = mybir.AluOpType
ACT = mybir.ActivationFunctionType

P = 128
D = 1024
S = 1024
FF = 2816
HALVES = 2
T = S // HALVES
TT = T // P
KD = D // P
KF = FF // P
DA = D // 2
KA = DA // P
HEADS = 8
HD = 64
CHUNK = 64
LEFT = 8
NBAND = LEFT * CHUNK // P + 1
BANDW = NBAND * P
MAX_REL = 128
EPS = 1e-6
NEG = -1e30

CW = KD * P
RAW = 2
RING = 4
OUT_BLOCKS = (8, 8, 6)
ADA_TILES = 3 * 3 * KD
ADA_FIRST = 20
ADA_GROUP = 4

PHASES = ["ffn", "ffn", "mix", "mix", "ffn", "ffn"]
IN_CHUNKS = {"ffn": 2 * KF, "mix": 24}
OUT_CHUNKS = {"ffn": 3 * KD, "mix": KD}
MIX_V, MIX_QK, MIX_CONV = 0, 4, 12
CHUNK_BASE = [sum(IN_CHUNKS[q] + OUT_CHUNKS[q] for q in PHASES[:p]) for p in range(len(PHASES))]
N_CHUNKS = sum(IN_CHUNKS[q] + OUT_CHUNKS[q] for q in PHASES)
NORM_TILES = [KD, KD, KD, KD, KA, KD, KA, KD, KD, KD]
NORM_OF_PHASE_OUT = [2, 3, 5, 7, 8, 9]
NORM_IN_PHASE = [1, 2, 3, 5, 7, 8]
NORM_CONV = {2: 4, 3: 6}

SM_C, SM_BADA, SM_GN, SM_GF, SM_QG, SM_KG, SM_WC, SM_BC, SM_GC = 0, 8, 80, 104, 112, 113, 114, 126, 130
SM_COLS = 134


def norm_sq(n):
    return sum(NORM_TILES[:n])


def norm_acc(n):
    return sum(1 + t for t in NORM_TILES[:n])


def build(nc, xT, w_ada, small, w_f1i, w_f1o, w_mix, w_mo, w_f2i, w_f2o, bias_ext, g_attn, out):
    base = (nc.sbuf_base + 31) // 32 * 32
    top = [0]

    def at(name, cols, dt, off):
        top[0] = max(top[0], off + cols * 4)
        return nc.alloc_sbuf_tensor_at(name, [P, cols], dt, offset=base + off)

    KB = 1024
    x = at("x", HALVES * KD * T, F32, 0)
    R_H = 32 * KB
    h_hi = at("h_hi", KD * T, F32R, R_H)
    h_lo = at("h_lo", KD * T, F32R, R_H + 16 * KB)
    R_HID = 64 * KB
    hid_hi = at("hid_hi", KF * T, F32R, R_HID)
    hid_lo = at("hid_lo", KF * T, F32R, R_HID + 44 * KB)
    R_W = 152 * KB
    raw = at("raw", RAW * CW, F32, R_W)
    w_hi = at("w_hi", RING * CW, F32R, R_W + 8 * KB)
    w_lo = at("w_lo", RING * CW, F32R, R_W + 24 * KB)
    R_T = 192 * KB
    sq = at("sq", T, F32, R_T)
    tmp = at("tmp", T, F32, R_T + 2 * KB)
    acc = at("acc", T, F32, R_T + 4 * KB)
    rstd = at("rstd", HALVES * T, F32, R_T + 6 * KB)
    ada_w = at("ada_w", CW, F32, R_T + 10 * KB)
    qsq = at("qsq", T, F32, R_T + 10 * KB)
    qrow = at("qrow", T, F32, R_T + 12 * KB)
    R_S = R_T + 14 * KB
    ident = at("ident", P, F32, R_S)
    sm = at("sm", SM_COLS, F32, R_S + 512)
    o = R_S + 512 + 544

    def tiny(name, cols):
        nonlocal o
        t = at(name, cols, F32, o)
        o += (cols * 4 + 31) // 32 * 32
        return t

    shift = tiny("shift", 3 * KD)
    a_scale = tiny("a_scale", 3 * KD)
    gate = tiny("gate", 3 * KD)
    s_c = tiny("s_c", KD)
    var = tiny("var", 8)
    rinv = tiny("rinv", 8)
    mhalf = tiny("mhalf", 8)
    one2 = tiny("one2", 3)
    nmax = tiny("nmax", 2)
    rsum = tiny("rsum", 2 * HEADS)
    rrec = tiny("rrec", HEADS)
    ssum = tiny("ssum", 1)
    yvar = tiny("yvar", 1)
    yr = tiny("yr", 1)
    qg = tiny("qg", 1)
    assert base + top[0] <= nc.sbuf_usable_end, (base + top[0], nc.sbuf_usable_end)

    ada0 = at("ada0", ADA_FIRST * CW, F32, R_HID)
    ada_acc = at("ada_acc", ADA_GROUP * P, F32, R_HID + 80 * KB)
    q_sb = at("q_sb", KA * T, F32, R_HID)
    k_sb = at("k_sb", KA * S, F32, R_HID + 8 * KB)
    v_sb = at("v_sb", (S // P) * DA, F32, R_HID + 24 * KB)
    yc = at("yc", KA * T, F32, R_HID + 40 * KB)
    y_hi = at("y_hi", KD * T, F32R, R_HID + 48 * KB)
    y_lo = at("y_lo", KD * T, F32R, R_HID + 64 * KB)
    cg = at("cg", KA * T, F32, R_HID + 48 * KB)
    UW = T + 2
    u_sb = at("u_sb", KA * UW, F32, R_HID + 56 * KB)
    ytok = at("ytok", DA, F32, R_HID + 80 * KB)
    g_row = at("g_row", DA, F32, R_HID + 82 * KB)
    halo = at("halo", KA * 2, F32, R_HID + 84 * KB)
    q_rev1 = at("q_rev1", KA * P, F32, R_HID + 84 * KB + 64)
    bias = at("bias", HEADS * BANDW, F32, R_H)
    s_sb = at("s_sb", 2 * BANDW, F32, R_H + 20 * KB)
    pT = at("pT", 2 * BANDW, F32, R_H + 25 * KB)
    q_rev0 = at("q_rev0", KA * P, F32, R_H + 30 * KB)
    q_rev = [q_rev0, q_rev1]
    out_sb = at("out_sb", KD * T, F32, R_H)
    out_sb1 = at("out_sb1", KD * T, F32, R_H + 16 * KB)

    def col(t, start, n):
        return t[:, bass.ds(start, n)]

    ctx = ExitStack()
    with ctx:
        pair = [ctx.enter_context(nc.psum_tensor(f"pair{i}", [P, 1024], F32)) for i in range(4)]
        bank = [pair[i // 2][:, (i % 2) * 512:(i % 2 + 1) * 512] for i in range(8)]
        tpair = pair[2]
        STAT, ADAB = 6, 7

        def sem(name):
            return ctx.enter_context(nc.semaphore(name))

        small_in = sem("small_in")
        x_in = [sem("x_in0"), sem("x_in1")]
        ada0_in = [sem(f"ada0_in{g}") for g in range(ADA_FIRST // ADA_GROUP)]
        raw_in = [sem(f"raw_in{i}") for i in range(RAW)]
        w_hi_done = sem("w_hi_done")
        w_ready = sem("w_ready")
        w_used = sem("w_used")
        gate_done = sem("gate_done")
        prod_done = sem("prod_done")
        hid_hi_done = sem("hid_hi_done")
        hid_done = sem("hid_done")
        x_done = sem("x_done")
        h_tmp = sem("h_tmp")
        h_hi_done = sem("h_hi_done")
        h_ready = sem("h_ready")
        sq_done = sem("sq_done")
        acc_done = sem("acc_done")
        stat_mm = sem("stat_mm")
        var_done = sem("var_done")
        pow_done = sem("pow_done")
        bc_done = sem("bc_done")
        rstd_done = sem("rstd_done")
        const_done = sem("const_done")
        sc_done = sem("sc_done")
        ada_chain = sem("ada_chain")
        ada_in = sem("ada_in")
        ada_pool = sem("ada_pool")
        ada_ready = sem("ada_ready")
        ada_mm = sem("ada_mm")
        mod_chain = sem("mod_chain")
        v_done = sem("v_done")
        qsq_done = sem("qsq_done")
        qst_mm = sem("qst_mm")
        qvar_done = sem("qvar_done")
        qpow_done = sem("qpow_done")
        qrow_done = sem("qrow_done")
        qbc_done = sem("qbc_done")
        qr_done = sem("qr_done")
        qk_done = sem("qk_done")
        cg_done = sem("cg_done")
        u_done = sem("u_done")
        cv_chain = sem("cv_chain")
        yc_done = sem("yc_done")
        halo_done = sem("halo_done")
        y_tmp = sem("y_tmp")
        y_hi_done = sem("y_hi_done")
        yc_ready = sem("yc_ready")
        grow_in = sem("grow_in")
        bias_in = [sem(f"bias_in{h}") for h in range(HEADS)]
        bias_ok = sem("bias_ok")
        qrev_done = sem("qrev_done")
        s_mm = sem("s_mm")
        s_done = sem("s_done")
        p_done = sem("p_done")
        t_mm = sem("t_mm")
        pt_done = sem("pt_done")
        pv_mm = sem("pv_mm")
        rrec_done = sem("rrec_done")
        yt_done = sem("yt_done")
        ysq_done = sem("ysq_done")
        yvar_done = sem("yvar_done")
        ypow_done = sem("ypow_done")
        yn_done = sem("yn_done")
        yT_mm = sem("yT_mm")
        ya_hi_done = sem("ya_hi_done")
        ya_ready = sem("ya_ready")
        out_done = sem("out_done")
        out_stored = sem("out_stored")
        CREDIT = 4

        block = ctx.enter_context(nc.Block())

        def wc(tap, ct):
            return sm[:, SM_WC + tap * KA + ct:SM_WC + tap * KA + ct + 1]

        def ph(p):
            return CHUNK_BASE[p], IN_CHUNKS[PHASES[p]], PHASES[p]

        J_BASE = {0: 0, 1: KF, 4: 2 * KF, 5: 3 * KF}
        ADA_IN_BASE = {0: ADA_FIRST, 1: ADA_FIRST + KF + KD}
        ADA_OUT_BASE = {0: ADA_FIRST + KF}
        MIX_NO = {2: 0, 3: 1}
        UNITS = TT * HEADS

        def spair(s):
            return pair[s % 2]

        def mod_col(sub, part, k):
            return (3 * sub + part) * KD + k

        @block.sync
        def _(sp):
            sp.dma_start(sm[:], small).then_inc(small_in, 16)

            def ada_load(g):
                src = w_ada[bass.ds(g * ADA_GROUP, ADA_GROUP)].rearrange("a p c -> p a c")
                dst = col(ada0, g * ADA_GROUP * CW, ADA_GROUP * CW).rearrange("p (a c) -> p a c", a=ADA_GROUP)
                sp.dma_start(dst, src).then_inc(ada0_in[g], 16)

            def load(n, src, cols, slot):
                if not (isinstance(n, int) and n < RAW):
                    sp.wait_ge(w_ready, n - RAW + 1)
                sp.dma_start(col(raw, slot * CW, cols), src).then_inc(raw_in[slot], 16)

            def chunk_src(w, i):
                return w[bass.ds(i, 1)].rearrange("a p c -> (a p) c")

            ada_load(0)
            sp.dma_start(col(x, 0, KD * T), xT[0]).then_inc(x_in[0], 16)
            for g in range(1, 4):
                ada_load(g)
            for c in range(RAW):
                load(c, chunk_src(w_f1i, c), CW, c)
            sp.dma_start(col(x, KD * T, KD * T), xT[1]).then_inc(x_in[1], 16)
            ada_load(4)
            for p in range(len(PHASES)):
                b, nin, kind = ph(p)
                win = {"ffn": w_f1i if p < 2 else w_f2i, "mix": w_mix}[kind]
                wout = {"ffn": w_f1o if p < 2 else w_f2o, "mix": w_mo}[kind]
                first = RAW if p == 0 else 0
                for c in range(first, 4 if first else 0):
                    load(b + c, chunk_src(win, c), CW, c % RAW)
                lo = 1 if first else 0
                with sp.Fori(lo, nin // 4) as i:
                    for c in range(4):
                        load(b + 4 * i + c, chunk_src(win, 4 * i + c), CW, c % RAW)
                if kind == "ffn":
                    with sp.Fori(0, 2) as i:
                        for m in range(4):
                            for c, nb in enumerate(OUT_BLOCKS):
                                e = 3 * m + c
                                src = wout[bass.ds(4 * i + m, 1), :, c * CW:c * CW + nb * P].rearrange("a p c -> (a p) c")
                                load(b + nin + 12 * i + e, src, nb * P, e % RAW)
                else:
                    with sp.Fori(0, 2) as i:
                        for m in range(4):
                            load(b + nin + 4 * i + m, chunk_src(wout, 4 * i + m), CW, m % RAW)

        @block.gpsimd
        def _(pool):
            nc.gpsimd.memset(ident[:], 0.0).then_inc(const_done, 1)
            nc.gpsimd.memset(mhalf[:], -0.5).then_inc(const_done, 1)
            nc.gpsimd.memset(one2[:], 1.0).then_inc(const_done, 1)
            pool.wait_ge(const_done, 3)
            nc.gpsimd.affine_select(out=ident[:], in_=ident[:], compare_op=ALU.not_equal, fill=1.0, base=0,
                                    pattern=[[-1, P]], channel_multiplier=1).then_inc(const_done, 1)
            pool.wait_ge(const_done, 4)
            nc.gpsimd.memset(one2[64:128, 1:2], 0.0).then_inc(const_done, 1)
            pool.wait_ge(const_done, 5)
            nc.gpsimd.memset(one2[0:64, 2:3], 0.0).then_inc(const_done, 1)

            def power(n):
                pool.wait_ge(var_done, n + 1)
                pool.wait_ge(bc_done, n) if n else None
                nc.gpsimd.tensor_tensor(rinv[:, 0:TT], var[:, 0:TT], mhalf[:, 0:TT], ALU.pow).then_inc(pow_done, 1)

            def ada_tile(f, k):
                pool.wait_ge(ada_mm, f)
                src = w_ada[bass.ds(f, 1)].rearrange("a p c -> (a p) c")
                pool.dma_start(ada_w[:], src).then_inc(ada_in, 16)
                pool.wait_ge(ada_in, 16 * k + 16)
                w3 = ada_w[:].rearrange("p (k c) -> p k c", k=KD)
                sc = bass.AP(s_c[:].tensor, s_c[:].offset, [list(s_c[:].ap[0]), [1, KD], [0, P]])
                nc.gpsimd.tensor_tensor(w3, w3, sc, ALU.mult).then_inc(ada_pool, 1)
                for e, w in enumerate((512, 256)):
                    pool.wait_ge(ada_pool, 3 * k + e + 1)
                    nc.gpsimd.tensor_tensor(ada_w[:, 0:w], ada_w[:, 0:w], ada_w[:, w:2 * w], ALU.add).then_inc(ada_pool, 1)
                pool.wait_ge(ada_pool, 3 * k + 3)
                nc.gpsimd.tensor_tensor(ada_w[:, 0:128], ada_w[:, 0:128], ada_w[:, 128:256], ALU.add).then_inc(ada_ready, 1)

            pool.wait_ge(const_done, 6)
            pool.wait_ge(sc_done, 1)
            power(0)
            for p in range(len(PHASES)):
                b, nin, kind = ph(p)
                if p in ADA_IN_BASE:
                    f0 = ADA_IN_BASE[p]
                    with pool.Fori(0, KF - 2) as j:
                        ada_tile(f0 + j, f0 - ADA_FIRST + j)
                    power(NORM_IN_PHASE[p])
                    with pool.Fori(KF - 2, KF) as j:
                        ada_tile(f0 + j, f0 - ADA_FIRST + j)
                if p in ADA_OUT_BASE:
                    f0 = ADA_OUT_BASE[p]
                    with pool.Fori(0, KD) as j:
                        ada_tile(f0 + j, f0 - ADA_FIRST + j)
                if kind == "ffn" and p > 1:
                    power(NORM_IN_PHASE[p])
                if kind == "mix":
                    mx = MIX_NO[p]
                    power(NORM_IN_PHASE[p])
                    for u in range(8):
                        g = 8 * mx + u
                        pool.wait_ge(qvar_done, g + 1)
                        pool.wait_ge(qbc_done, g) if g else None
                        pool.wait_ge(bc_done, NORM_IN_PHASE[p] + 1) if u == 0 else None
                        nc.gpsimd.tensor_tensor(rinv[:], var[:], mhalf[:], ALU.pow).then_inc(qpow_done, 1)
                        pool.wait_ge(qpow_done, g + 1)
                        wide = bass.AP(rinv[:].tensor, rinv[:].offset, [list(rinv[:].ap[0]), [1, 2 * TT], [0, HD]])
                        nc.gpsimd.tensor_copy(qrow[:].rearrange("p (r d) -> p r d", d=HD), wide).then_inc(qrow_done, 1)
                    pool.wait_ge(w_used, b + MIX_CONV + 12)
                    if mx == 0:
                        g0 = bass.AP(g_attn.tensor, 0, [[0, P], [1, DA]])
                        pool.dma_start(g_row[:], g0).then_inc(grow_in, 16)
                    for h in range(HEADS):
                        src = bass.AP(bias_ext.tensor, h * (BANDW + P - 1), [[1, P], [1, BANDW]])
                        pool.dma_start(col(bias, h * BANDW, BANDW), src).then_inc(bias_in[h], 16)

                    def reverse_q(qt):
                        n = TT * mx + qt
                        if qt == 0:
                            pool.wait_ge(qk_done, 8 * (mx + 1))
                        if qt >= 2:
                            pool.wait_ge(s_mm, UNITS * mx + HEADS * (qt - 1))
                        src = bass.AP(q_sb[:].tensor, q_sb[:].offset + qt * P + P - 1,
                                      [list(q_sb[:].ap[0]), [T, KA], [-1, P]])
                        nc.gpsimd.tensor_copy(q_rev[qt % 2][:].rearrange("p (t c) -> p t c", t=KA), src)\
                            .then_inc(qrev_done, 1)
                    reverse_q(0)
                    power(NORM_CONV[p])
                    pool.wait_ge(pow_done, NORM_CONV[p] + 1)
                    for h in range(HEADS):
                        pool.wait_ge(bias_in[h], 16 * (mx + 1))
                        if h:
                            pool.wait_ge(bias_ok, 2 * (HEADS * mx + h))
                        nc.gpsimd.memset(bias[64:128, h * BANDW + BANDW - 64:h * BANDW + BANDW], NEG).then_inc(bias_ok, 1)
                        pool.wait_ge(bias_ok, 2 * (HEADS * mx + h) + 1)
                        nc.gpsimd.memset(bias[0:64, h * BANDW:h * BANDW + 64], NEG).then_inc(bias_ok, 1)
                    pool.wait_ge(bias_ok, 2 * HEADS * (mx + 1))
                    reverse_q(1)
                    for qt in range(TT):
                        if 2 <= qt + 1 < TT:
                            reverse_q(qt + 1)
                        n = TT * mx + qt
                        pool.wait_ge(yvar_done, n + 1)
                        nc.gpsimd.tensor_tensor(yr[:], yvar[:], mhalf[:, 0:1], ALU.pow).then_inc(ypow_done, 1)
            power(9)

        @block.scalar
        def _(act):
            def split_hi(nb, k, c):
                n = nb + c
                slot = n % RING
                act.wait_ge(raw_in[n % RAW], 16 * (n // RAW + 1) + 8 * k)
                if not (isinstance(k, int) and n + k < RING):
                    act.wait_ge(w_used, n - RING + 1 + k)
                nc.scalar.copy(col(w_hi, slot * CW, CW), col(raw, (n % RAW) * CW, CW)).then_inc(w_hi_done, 1)

            def square(src, n, t):
                s = norm_sq(n) + t
                a = norm_acc(n) + 1 + t
                if isinstance(t, int) and t == 0 and n > 0:
                    a = norm_acc(n)
                if not (isinstance(t, int) and s == 0):
                    act.wait_ge(acc_done, a)
                nc.scalar.activation(sq[:], src, ACT.Square).then_inc(sq_done, 1)

            def spread(n, dst):
                act.wait_ge(bc_done, n + 1)
                nc.scalar.copy(dst, bank[STAT][:]).then_inc(rstd_done, 1)

            def h_part(ne, m, sub):
                act.wait_ge(h_tmp, KD * ne + m + 1)
                nc.scalar.activation(col(h_hi, m * T, T), tmp[:], ACT.Identity,
                                     bias=shift[:, bass.ds(sub * KD + m, 1)]).then_inc(h_hi_done, 1)

            def store(m):
                act.wait_ge(out_done, m + 1)
                src = col(out_sb if m < KD else out_sb1, (m % KD) * T, T)
                act.dma_start(out[m], src).then_inc(out_stored, 16)

            act.wait_ge(small_in, 16)
            nc.scalar.activation(s_c[:], sm[:, SM_C:SM_C + KD], ACT.Silu).then_inc(sc_done, 1)
            split_hi(0, 0, 0)
            split_hi(0, 0, 1)
            for hf in range(HALVES):
                act.wait_ge(x_in[hf], 16)
                for t in range(KD):
                    square(col(x, (hf * KD + t) * T, T), hf, t)
                if hf == 0:
                    spread(0, col(rstd, 0, T))
                    for m in range(KD):
                        h_part(0, m, 0)
                    split_hi(0, 0, 2)
                    split_hi(0, 0, 3)

            def ffn_in(p, i, jj):
                b, j0 = CHUNK_BASE[p], J_BASE[p]
                n, jl = b + 2 * jj, j0 + jj
                act.wait_ge(w_used, n + 1 + 4 * i)
                act.wait_ge(prod_done, CREDIT + jl + 2 * i)
                nc.scalar.activation(sq[:], bank[jj][:], ACT.Silu).then_inc(gate_done, 1)
                split_hi(b + RING, 4 * i, 2 * jj)
                split_hi(b + RING, 4 * i, 2 * jj + 1)
                act.wait_ge(prod_done, CREDIT + jl + 1 + 2 * i)
                nc.scalar.copy(col(hid_hi, (2 * i + jj) * T, T), tmp[:]).then_inc(hid_hi_done, 1)

            def side(p, m):
                if p + 1 < len(PHASES):
                    h_part(p + 1, m, (p + 1) // 2)

            def out_tile(p, i, m, last):
                b, nin, kind = ph(p)
                per = 3 if kind == "ffn" else 1
                k = 4 * per * i
                n = b + nin + per * m
                for c in range(per):
                    if c == 1:
                        side(p, 4 * i + m)
                    if not (last and per * m + c >= 4 * per - RING):
                        split_hi(n + RING, k, c)
                if per == 1:
                    side(p, 4 * i + m)
                act.wait_ge(x_done, CREDIT + KD * p + m + 1 + 4 * i)
                square(col(x, ((p % 2) * KD + m + 4 * i) * T, T), NORM_OF_PHASE_OUT[p], 4 * i + m)
                if p + 1 == len(PHASES):
                    store(4 * i + m)

            for p in range(len(PHASES)):
                b, nin, kind = ph(p)
                nrm = NORM_IN_PHASE[p]
                if kind == "ffn":
                    act.wait_ge(acc_done, norm_acc(nrm) + 1 + NORM_TILES[nrm])
                    with act.Fori(0, KF // 2 - 1) as i:
                        for jj in range(2):
                            ffn_in(p, i, jj)
                    for jj in range(2):
                        ffn_in(p, KF // 2 - 1, jj)
                    spread(nrm, col(rstd, ((p + 1) % 2) * T, T))
                else:
                    mx = MIX_NO[p]
                    for c in range(4):
                        split_hi(b + RING, 0, c)
                    for t in range(TT):
                        act.wait_ge(w_used, b + MIX_QK)
                        nc.scalar.copy(col(v_sb, (TT * mx + t) * DA, DA), bank[4 + t][:]).then_inc(v_done, 1)

                    def qk_square(u):
                        g = 8 * mx + u
                        act.wait_ge(w_used, b + MIX_QK + u + 1)
                        act.wait_ge(qst_mm, g) if g else None
                        nc.scalar.activation(qsq[:], bank[u % 4][:], ACT.Square).then_inc(qsq_done, 1)

                    def qk_spread(u):
                        g = 8 * mx + u
                        act.wait_ge(qbc_done, g + 1)
                        act.wait_ge(qk_done, g) if g else None
                        nc.scalar.copy(sq[:], bank[5][:]).then_inc(qr_done, 1)

                    for u in range(8):
                        qk_square(u)
                        split_hi(b + RING + MIX_QK, 0, u)
                        if u == 1:
                            spread(nrm, col(rstd, ((p + 1) % 2) * T, T))
                        if u >= 2:
                            qk_spread(u - 2)
                    for c in range(12):
                        if c < 4:
                            act.wait_ge(w_used, b + MIX_CONV + c + 1)
                            nc.scalar.copy(col(cg, c * T, T), bank[c][:]).then_inc(cg_done, 1)
                            if c < 2:
                                qk_spread(6 + c)
                        split_hi(b + RING + MIX_CONV, 0, c)
                        if c >= 8:
                            ct = c - 8
                            act.wait_ge(yc_done, KA * mx + ct + 1)
                            square(col(yc, ct * T, T), NORM_CONV[p], ct)
                    spread(NORM_CONV[p], col(rstd, (p % 2) * T, T))
                    for ct in range(KA):
                        act.wait_ge(y_tmp, KA * mx + ct + 1)
                        nc.scalar.copy(col(y_hi, (KA + ct) * T, T), tmp[:]).then_inc(y_hi_done, 1)

                    def softmax(s):
                        qt, h = s // HEADS, s % HEADS
                        nb = min(NBAND, TT * mx + qt + 1)
                        g = UNITS * mx + s
                        act.wait_ge(s_done, g + 1)
                        if h == 0 and TT * mx + qt >= 2:
                            act.wait_ge(rrec_done, TT * mx + qt - 1)
                        sl = s_sb[:, (s % 2) * BANDW:(s % 2) * BANDW + nb * P]
                        r = (qt % 2) * HEADS + h
                        nc.scalar.activation(sl, sl, ACT.Exp, scale=-1.0, bias=nmax[:, s % 2:s % 2 + 1],
                                             accum_out=rsum[:, r:r + 1]).then_inc(p_done, 1)

                    def y_square(qt):
                        n = TT * mx + qt
                        act.wait_ge(yt_done, n + 1)
                        act.wait_ge(yvar_done, n) if n else None
                        nc.scalar.activation(sq[:], ytok[:], ACT.Square, accum_out=ssum[:]).then_inc(ysq_done, 1)

                    def y_split(qt):
                        n = TT * mx + qt
                        act.wait_ge(yT_mm, n + 1)
                        yb = bank[6 + qt % 2]
                        src = bass.AP(yb[:].tensor, yb[:].offset + P - 1, [list(yb[:].ap[0]), [P, KA], [-1, P]])
                        dst = y_hi[:, 0:KA * T].rearrange("p (t c) -> p t c", t=KA)[:, :, qt * P:(qt + 1) * P]
                        nc.scalar.copy(dst, src).then_inc(ya_hi_done, 1)

                    for s in range(UNITS):
                        softmax(s)
                        if s % HEADS == 4 and s > HEADS:
                            y_square(s // HEADS - 1)
                        if s % HEADS == 7 and s > HEADS:
                            y_split(s // HEADS - 1)
                    y_square(TT - 1)
                    y_split(TT - 1)
                if p + 1 < len(PHASES):
                    with act.Fori(0, 2) as i:
                        for m in range(4):
                            out_tile(p, i, m, False)
                else:
                    for i in range(2):
                        for m in range(4):
                            out_tile(p, i, m, i == 1)
            spread(9, col(rstd, T, T))
            for m in range(KD, HALVES * KD):
                store(m)
            act.wait_ge(out_stored, 16 * HALVES * KD)

        @block.vector
        def _(dve):
            nc.vector.memset(var[:], 0.0).then_inc(gate_done, CREDIT)
            nc.vector.memset(nmax[:], 0.0).then_inc(prod_done, CREDIT)
            nc.vector.memset(yvar[:], 0.0).then_inc(x_done, CREDIT)
            nc.vector.memset(rrec[:], 0.0).then_inc(hid_done, CREDIT)
            nc.vector.memset(acc[:], 0.0).then_inc(acc_done, 1)

            def split_lo(nb, k, c):
                n = nb + c
                slot = n % RING
                dve.wait_ge(w_hi_done, n + 1 + k)
                nc.vector.tensor_tensor(col(w_lo, slot * CW, CW), col(raw, (n % RAW) * CW, CW),
                                        col(w_hi, slot * CW, CW).bitcast(F32), ALU.subtract).then_inc(w_ready, 1)

            def add_square(n, t):
                dve.wait_ge(sq_done, norm_sq(n) + t + 1)
                dve.wait_ge(acc_done, norm_acc(n) + t + 1)
                nc.vector.tensor_tensor(acc[:], acc[:], sq[:], ALU.add).then_inc(acc_done, 1)

            def mean(n):
                width = NORM_TILES[n] * P
                dve.wait_ge(stat_mm, n + 1)
                if n:
                    dve.wait_ge(pow_done, n)
                if n in (4, 6):
                    dve.wait_ge(qpow_done, 4 * n - 8)
                nc.vector.tensor_scalar(var[:, 0:TT], bank[STAT][:, 0:TT], 1.0 / width, EPS,
                                        ALU.mult, ALU.add).then_inc(var_done, 1)
                if n < 9:
                    nc.vector.memset(acc[:], 0.0).then_inc(acc_done, 1)

            def h_first(ne, m, sub, hf):
                g = KD * ne + m
                if not (isinstance(m, int) and g == 0):
                    dve.wait_ge(h_ready, g)
                nc.vector.scalar_tensor_tensor(tmp[:], col(x, (hf * KD + m) * T, T),
                                               a_scale[:, bass.ds(sub * KD + m, 1)], col(rstd, hf * T, T),
                                               ALU.mult, ALU.mult).then_inc(h_tmp, 1)

            def h_second(ne, m, sub):
                dve.wait_ge(h_hi_done, KD * ne + m + 1)
                nc.vector.scalar_tensor_tensor(col(h_lo, m * T, T), tmp[:], shift[:, bass.ds(sub * KD + m, 1)],
                                               col(h_hi, m * T, T).bitcast(F32), ALU.add, ALU.subtract)\
                    .then_inc(h_ready, 1)

            chain = [0]

            def link(ins):
                chain[0] += 1
                ins.then_inc(mod_chain, 1)
                dve.wait_ge(mod_chain, chain[0])

            def modulation(sub, parts):
                for part in parts:
                    f = mod_col(sub, part, 0)
                    src, b_ = bank[ADAB][:, f:f + KD], sm[:, SM_BADA + f:SM_BADA + f + KD]
                    if part == 0:
                        link(nc.vector.tensor_tensor(shift[:, sub * KD:(sub + 1) * KD], src, b_, ALU.add))
                    if part == 1:
                        d = a_scale[:, sub * KD:(sub + 1) * KD]
                        link(nc.vector.tensor_tensor(d, src, b_, ALU.add))
                        link(nc.vector.scalar_tensor_tensor(d, d, 1.0, sm[:, SM_GN + sub * KD:SM_GN + (sub + 1) * KD],
                                                            ALU.add, ALU.mult))
                    if part == 2:
                        d = gate[:, sub * KD:(sub + 1) * KD]
                        link(nc.vector.tensor_tensor(d, src, b_, ALU.add))
                        w = 1.0 if sub == 1 else 0.5
                        link(nc.vector.tensor_scalar(d, d, 1.0, w, ALU.add, ALU.mult))

            dve.wait_ge(sc_done, 1)
            nc.vector.tensor_scalar(qg[:], sm[:, SM_QG:SM_QG + 1], HD ** -0.5, None, ALU.mult)

            def ada_first(g):
                dve.wait_ge(ada0_in[g], 16)
                if g:
                    dve.wait_ge(ada_mm, ADA_GROUP * g)
                w4 = col(ada0, g * ADA_GROUP * CW, ADA_GROUP * CW).rearrange("p (a k c) -> p a k c", a=ADA_GROUP, k=KD)
                a3 = ada_acc[:].rearrange("p (a c) -> p a c", a=ADA_GROUP)
                nc.vector.tensor_scalar(a3, w4[:, :, 0, :], s_c[:, 0:1], None, ALU.mult).then_inc(ada_chain, 1)
                for k in range(1, KD):
                    dve.wait_ge(ada_chain, KD * g + k)
                    nc.vector.scalar_tensor_tensor(a3, w4[:, :, k, :], s_c[:, k:k + 1], a3,
                                                   ALU.mult, ALU.add).then_inc(ada_chain, 1)

            ada_first(0)
            split_lo(0, 0, 0)
            split_lo(0, 0, 1)
            ada_first(1)
            for t in range(KD):
                add_square(0, t)
            mean(0)
            ada_first(2)
            ada_first(3)
            dve.wait_ge(ada_mm, 16)
            modulation(0, (0, 1))
            dve.wait_ge(rstd_done, 1)
            for m in range(KD):
                h_first(0, m, 0, 0)
                h_second(0, m, 0)
            split_lo(0, 0, 2)
            split_lo(0, 0, 3)
            ada_first(4)
            for t in range(KD):
                add_square(1, t)

            def ffn_in(p, i, jj):
                b, j0 = CHUNK_BASE[p], J_BASE[p]
                jl = j0 + jj
                split_lo(b + RING, 4 * i, 2 * jj)
                dve.wait_ge(gate_done, CREDIT + jl + 1 + 2 * i)
                dve.wait_ge(w_used, b + 2 * jj + 2 + 4 * i)
                dve.wait_ge(hid_done, CREDIT + jl + 2 * i)
                nc.vector.tensor_tensor(tmp[:], sq[:], bank[2 + jj][:], ALU.mult).then_inc(prod_done, 1)
                split_lo(b + RING, 4 * i, 2 * jj + 1)
                dve.wait_ge(hid_hi_done, jl + 1 + 2 * i)
                hj = (2 * i + jj) * T
                nc.vector.tensor_tensor(col(hid_lo, hj, T), tmp[:], col(hid_hi, hj, T).bitcast(F32), ALU.subtract)\
                    .then_inc(hid_done, 1)

            def side_first(p, m):
                if p + 1 < len(PHASES):
                    h_first(p + 1, m, (p + 1) // 2, (p + 1) % 2)

            def side_second(p, m):
                if p + 1 < len(PHASES):
                    h_second(p + 1, m, (p + 1) // 2)
                else:
                    final(m, 0, out_sb)

            def final(m, hf, dst):
                nc.vector.scalar_tensor_tensor(col(dst, m * T, T), col(x, (hf * KD + m) * T, T),
                                               sm[:, SM_GF + m:SM_GF + m + 1], col(rstd, hf * T, T),
                                               ALU.mult, ALU.mult).then_inc(out_done, 1)

            def out_tile(p, i, m, last):
                b, nin, kind = ph(p)
                per = 3 if kind == "ffn" else 1
                k = 4 * per * i
                n = b + nin + per * m
                hf, sub = p % 2, p // 2

                def split_c(c):
                    if not (last and per * m + c >= 4 * per - RING):
                        split_lo(n + RING, k, c)

                split_c(0)
                side_first(p, 4 * i + m)
                if per == 3:
                    split_c(1)
                side_second(p, 4 * i + m)
                dve.wait_ge(w_used, n + per + k)
                xt = col(x, (hf * KD + m + 4 * i) * T, T)
                nc.vector.scalar_tensor_tensor(xt, bank[m][:], gate[:, bass.ds(sub * KD + m + 4 * i, 1)], xt,
                                               ALU.mult, ALU.add).then_inc(x_done, 1)
                if per == 3:
                    split_c(2)
                add_square(NORM_OF_PHASE_OUT[p], 4 * i + m)

            for p in range(len(PHASES)):
                b, nin, kind = ph(p)
                nrm = NORM_IN_PHASE[p]
                dve.wait_ge(h_ready, KD * (p + 1))
                if kind == "ffn":
                    with dve.Fori(0, KF // 2 - 1) as i:
                        for jj in range(2):
                            ffn_in(p, i, jj)
                    mean(nrm)
                    for jj in range(2):
                        ffn_in(p, KF // 2 - 1, jj)
                    if p == 0:
                        dve.wait_ge(ada_mm, ADA_FIRST + KF)
                        modulation(0, (2,))
                        modulation(1, (0, 1))
                    if p == 1:
                        dve.wait_ge(ada_mm, ADA_TILES)
                        modulation(1, (2,))
                        modulation(2, (0, 1, 2))
                    dve.wait_ge(rstd_done, {0: 2, 1: 3, 4: 8, 5: 9}[p])
                else:
                    mx = MIX_NO[p]
                    for c in range(4):
                        split_lo(b + RING, 0, c)
                    mean(nrm)

                    def qk_mean(u):
                        g = 8 * mx + u
                        dve.wait_ge(qst_mm, g + 1)
                        if g:
                            dve.wait_ge(qpow_done, g)
                        if u == 0:
                            dve.wait_ge(pow_done, nrm + 1)
                        nc.vector.tensor_scalar(var[:], bank[4][:, 0:8], 1.0 / HD, EPS, ALU.mult, ALU.add)\
                            .then_inc(qvar_done, 1)

                    def qk_scale(u):
                        g, t = 8 * mx + u, u // 2
                        dve.wait_ge(qr_done, g + 1)
                        if u % 2 == 0:
                            dst, gc = col(q_sb, t * T, T), qg[:, 0:1]
                        else:
                            dst, gc = col(k_sb, t * S + mx * T, T), sm[:, SM_KG:SM_KG + 1]
                        nc.vector.scalar_tensor_tensor(dst, bank[u % 4][:], gc, sq[:], ALU.mult, ALU.mult)\
                            .then_inc(qk_done, 1)

                    for u in range(8):
                        split_lo(b + RING + MIX_QK, 0, u)
                        if u >= 1:
                            qk_mean(u - 1)
                        if u >= 2:
                            qk_scale(u - 2)
                    for c in range(12):
                        ct = c % 4
                        if c < 2:
                            if c == 0:
                                qk_mean(7)
                            qk_scale(6 + c)
                        split_lo(b + RING + MIX_CONV, 0, c)
                        ug = col(u_sb, ct * UW, UW)
                        cgt = col(cg, ct * T, T)
                        cv = 4 * (KA * mx + ct)
                        if 4 <= c < 8:
                            if mx == 0:
                                nc.vector.memset(ug[:, 0:2], 0.0).then_inc(halo_done, 1)
                            else:
                                nc.vector.tensor_copy(ug[:, 0:2], halo[:, 2 * ct:2 * ct + 2]).then_inc(halo_done, 1)
                            dve.wait_ge(cg_done, KA * mx + ct + 1)
                            dve.wait_ge(w_used, b + MIX_CONV + c + 1)
                            nc.vector.tensor_tensor(ug[:, 2:UW], bank[ct][:], cgt, ALU.mult).then_inc(cv_chain, 1)
                            dve.wait_ge(halo_done, 2 * KA * mx + ct + 1)
                            dve.wait_ge(cv_chain, cv + 1)
                            nc.vector.tensor_scalar(cgt, ug[:, 2:UW], wc(2, ct), sm[:, SM_BC + ct:SM_BC + ct + 1],
                                                    ALU.mult, ALU.add).then_inc(cv_chain, 1)
                            for tap in (1, 0):
                                dve.wait_ge(cv_chain, cv + 3 - tap)
                                nc.vector.scalar_tensor_tensor(cgt, ug[:, tap:tap + T], wc(tap, ct), cgt,
                                                               ALU.mult, ALU.add).then_inc(cv_chain, 1)
                        if c >= 8:
                            dve.wait_ge(w_used, b + MIX_CONV + c + 1)
                            dve.wait_ge(cv_chain, cv + 4)
                            nc.vector.tensor_tensor(col(yc, ct * T, T), bank[ct][:], cgt, ALU.mult).then_inc(yc_done, 1)
                            if mx == 0:
                                nc.vector.tensor_copy(halo[:, 2 * ct:2 * ct + 2], ug[:, T:UW]).then_inc(halo_done, 1)
                            if ct >= 1:
                                add_square(NORM_CONV[p], ct - 1)
                    add_square(NORM_CONV[p], 3)

                    def conv_split():
                        dve.wait_ge(rstd_done, NORM_CONV[p] + 1)
                        for ct in range(KA):
                            g = KA * mx + ct
                            if g:
                                dve.wait_ge(yc_ready, g)
                            nc.vector.scalar_tensor_tensor(tmp[:], col(yc, ct * T, T), sm[:, SM_GC + ct:SM_GC + ct + 1],
                                                           col(rstd, (p % 2) * T, T), ALU.mult, ALU.mult).then_inc(y_tmp, 1)
                            dve.wait_ge(y_hi_done, g + 1)
                            yl = (KA + ct) * T
                            nc.vector.tensor_tensor(col(y_lo, yl, T), tmp[:], col(y_hi, yl, T).bitcast(F32),
                                                    ALU.subtract).then_inc(yc_ready, 1)
                    mean(NORM_CONV[p])
                    conv_split()

                    def scores(s):
                        qt, h = s // HEADS, s % HEADS
                        nb = min(NBAND, TT * mx + qt + 1)
                        g = UNITS * mx + s
                        dve.wait_ge(s_mm, g + 1)
                        if g >= 2:
                            dve.wait_ge(t_mm, g - 1)
                        if qt == 0:
                            dve.wait_ge(bias_ok, 2 * (HEADS * mx + h + 1))
                        off = (s % 2) * BANDW
                        nc.vector.tensor_tensor_reduce(
                            out=s_sb[:, off:off + nb * P], in0=spair(s)[:, 0:nb * P],
                            in1=bias[:, (h + 1) * BANDW - nb * P:(h + 1) * BANDW],
                            scale=-1.0, scalar=3e38, op0=ALU.add, op1=ALU.min,
                            accum_out=nmax[:, s % 2:s % 2 + 1]).then_inc(s_done, 1)

                    def probs(s):
                        qt = s // HEADS
                        nb = min(NBAND, TT * mx + qt + 1)
                        g = UNITS * mx + s
                        dve.wait_ge(t_mm, g + 1)
                        if g >= 2:
                            dve.wait_ge(pv_mm, g - 1)
                        off = (s % 2) * BANDW
                        nc.vector.tensor_copy(pT[:, off:off + nb * P], tpair[:, 0:nb * P]).then_inc(pt_done, 1)

                    def y_rows(qt):
                        n = TT * mx + qt
                        dve.wait_ge(pv_mm, UNITS * mx + HEADS * (qt + 1))
                        r = (qt % 2) * HEADS
                        if n:
                            dve.wait_ge(yt_done, n)
                        nc.vector.reciprocal(rrec[:], rsum[:, r:r + HEADS]).then_inc(rrec_done, 1)
                        dve.wait_ge(rrec_done, n + 1)
                        if n:
                            dve.wait_ge(yT_mm, n)
                        rb = bass.AP(rrec[:].tensor, rrec[:].offset, [list(rrec[:].ap[0]), [1, HEADS], [0, HD]])
                        nc.vector.tensor_tensor(ytok[:].rearrange("p (h d) -> p h d", h=HEADS),
                                                bank[6 + qt % 2][:].rearrange("p (h d) -> p h d", h=HEADS), rb,
                                                ALU.mult).then_inc(yt_done, 1)

                    def y_norm(qt):
                        n = TT * mx + qt
                        dve.wait_ge(ysq_done, n + 1)
                        if n:
                            dve.wait_ge(ypow_done, n)
                        nc.vector.tensor_scalar(yvar[:], ssum[:], 1.0 / DA, EPS, ALU.mult, ALU.add).then_inc(yvar_done, 1)

                    def y_norm2(qt):
                        n = TT * mx + qt
                        dve.wait_ge(ypow_done, n + 1)
                        dve.wait_ge(grow_in, 16)
                        nc.vector.scalar_tensor_tensor(ytok[:], ytok[:], yr[:, 0:1], g_row[:], ALU.mult, ALU.mult)\
                            .then_inc(yn_done, 1)

                    def y_low(qt):
                        n = TT * mx + qt
                        dve.wait_ge(ya_hi_done, n + 1)
                        yb = bank[6 + qt % 2]
                        src = bass.AP(yb[:].tensor, yb[:].offset + P - 1, [list(yb[:].ap[0]), [P, KA], [-1, P]])
                        sl = slice(qt * P, (qt + 1) * P)
                        hi = y_hi[:, 0:KA * T].rearrange("p (t c) -> p t c", t=KA)[:, :, sl]
                        lo = y_lo[:, 0:KA * T].rearrange("p (t c) -> p t c", t=KA)[:, :, sl]
                        nc.vector.tensor_tensor(lo, src, hi.bitcast(F32), ALU.subtract).then_inc(ya_ready, 1)

                    for s in range(UNITS + 3):
                        if s < UNITS:
                            scores(s)
                        if 2 <= s < UNITS + 2:
                            probs(s - 2)
                        if s > HEADS:
                            qt = s // HEADS - 1
                            if s % HEADS == 3:
                                y_rows(qt)
                            if s % HEADS == 4 and s < UNITS:
                                y_norm(qt)
                            if s % HEADS == 5 and s < UNITS:
                                y_norm2(qt)
                            if s % HEADS == 7 and s < UNITS:
                                y_low(qt)
                    y_rows(TT - 1)
                    y_norm(TT - 1)
                    y_norm2(TT - 1)
                    y_low(TT - 1)
                if kind == "ffn":
                    dve.wait_ge(hid_done, CREDIT + J_BASE[p] + KF)
                else:
                    dve.wait_ge(yc_ready, KA * (mx + 1))
                if p + 1 < len(PHASES):
                    with dve.Fori(0, 2) as i:
                        for m in range(4):
                            out_tile(p, i, m, False)
                else:
                    for i in range(2):
                        for m in range(4):
                            out_tile(p, i, m, i == 1)
            mean(9)
            dve.wait_ge(rstd_done, 10)
            for m in range(KD):
                final(m, 1, out_sb1)

        @block.tensor
        def _(pe):
            def passes(dst, lh, ll, rh, rl, first, last):
                nc.tensor.matmul(dst, lh, rh, start=first, stop=False)
                nc.tensor.matmul(dst, lh, rl, start=False, stop=False)
                return nc.tensor.matmul(dst, ll, rh, start=False, stop=last)

            def w_block(slot, k):
                c = slot * CW + k * P
                return w_hi[:, c:c + P], w_lo[:, c:c + P]

            def act_tile(hi, lo, k):
                return hi[:, k * T:(k + 1) * T], lo[:, k * T:(k + 1) * T]

            def norm_stats(n):
                pe.wait_ge(acc_done, norm_acc(n) + 1 + NORM_TILES[n])
                for t in range(TT):
                    mm = nc.tensor.matmul(bank[STAT][:, t:t + 1], acc[:, t * P:(t + 1) * P], one2[:, 0:1],
                                          start=True, stop=True)
                mm.then_inc(stat_mm, 1)

            def norm_spread(n):
                pe.wait_ge(pow_done, n + 1)
                for t in range(TT):
                    r = rinv[:, t:t + 1]
                    src = bass.AP(r.tensor, r.offset, [list(r.ap[0]), [0, P]])
                    mm = nc.tensor.transpose(bank[STAT][:, t * P:(t + 1) * P], src, ident[:])
                mm.then_inc(bc_done, 1)

            def ada_column(f, src, k):
                return nc.tensor.matmul(bank[ADAB][:, bass.ds(f, 1)], src[:, k * P:(k + 1) * P], one2[:, 0:1],
                                        start=True, stop=True)

            pe.wait_ge(const_done, 6)
            for g in range(2):
                pe.wait_ge(ada_chain, KD * (g + 1))
                for k in range(ADA_GROUP):
                    ada_column(ADA_GROUP * g + k, ada_acc, k).then_inc(ada_mm, 1)
            norm_stats(0)
            pe.wait_ge(ada_chain, KD * 3)
            for k in range(ADA_GROUP):
                ada_column(8 + k, ada_acc, k).then_inc(ada_mm, 1)
            norm_spread(0)
            pe.wait_ge(ada_chain, KD * 4)
            for k in range(ADA_GROUP):
                ada_column(12 + k, ada_acc, k).then_inc(ada_mm, 1)

            def ffn_in(p, i, jj):
                b, j0 = CHUNK_BASE[p], J_BASE[p]
                for part in range(2):
                    c = 2 * jj + part
                    pe.wait_ge(w_ready, b + c + 1 + 4 * i)
                    pe.wait_ge(gate_done if part == 0 else prod_done, CREDIT - 1 + j0 + jj + 2 * i)
                    if part == 1 and jj == 1:
                        pe.wait_ge(x_done, CREDIT + KD * p)
                    dst = bank[2 * part + jj]
                    for k in range(KD):
                        mm = passes(dst[:], *w_block(c, k), *act_tile(h_hi, h_lo, k), k == 0, k == KD - 1)
                    mm.then_inc(w_used, 1)
                if p == 0 and jj == 0 and isinstance(i, int) and i == 0:
                    pe.wait_ge(ada_chain, KD * 5)
                    pe.wait_ge(mod_chain, 3)
                    for k in range(ADA_GROUP):
                        ada_column(4 * ADA_GROUP + k, ada_acc, k).then_inc(ada_mm, 1)
                if p in ADA_IN_BASE:
                    f = ADA_IN_BASE[p] + jj + 2 * i
                    pe.wait_ge(ada_ready, f - ADA_FIRST + 1)
                    ada_column(f, ada_w, 0).then_inc(ada_mm, 1)

            for p in range(len(PHASES)):
                b, nin, kind = ph(p)
                nrm = NORM_IN_PHASE[p]
                pe.wait_ge(h_ready, KD * (p + 1))
                if p:
                    pe.wait_ge(x_done, CREDIT + KD * p - 1)
                if kind == "ffn":
                    if p == 0:
                        for jj in range(2):
                            ffn_in(p, 0, jj)
                    with pe.Fori(1 if p == 0 else 0, KF // 2 - 1) as i:
                        for jj in range(2):
                            ffn_in(p, i, jj)
                    norm_stats(nrm)
                    for jj in range(2):
                        ffn_in(p, KF // 2 - 1, jj)
                    norm_spread(nrm)
                    pe.wait_ge(gate_done, CREDIT + J_BASE[p] + KF - 1)

                    def out_col(p, i, m):
                        n = b + nin + 3 * m
                        k = 0
                        for c, nb in enumerate(OUT_BLOCKS):
                            pe.wait_ge(w_ready, n + c + 1 + 12 * i)
                            pe.wait_ge(hid_done, CREDIT + J_BASE[p] + (16 if c < 2 else KF))
                            if c == 0:
                                pe.wait_ge(x_done, CREDIT + KD * p + m - 3 + 4 * i)
                            for e in range(nb):
                                mm = passes(bank[m][:], *w_block((3 * m + c) % RING, e), *act_tile(hid_hi, hid_lo, k),
                                            k == 0, k == KF - 1)
                                k += 1
                            mm.then_inc(w_used, 1)
                        if p in ADA_OUT_BASE:
                            f = ADA_OUT_BASE[p] + m + 4 * i
                            pe.wait_ge(mod_chain, 8)
                            pe.wait_ge(ada_ready, f - ADA_FIRST + 1)
                            ada_column(f, ada_w, 0).then_inc(ada_mm, 1)
                    with pe.Fori(0, 2) as i:
                        for m in range(4):
                            out_col(p, i, m)
                else:
                    mx = MIX_NO[p]
                    for c in range(4):
                        pe.wait_ge(w_ready, b + c + 1)
                        for kk in range(2):
                            k = 2 * c + kk
                            wh = w_hi[:, c * CW + kk * DA:c * CW + (kk + 1) * DA]
                            wl = w_lo[:, c * CW + kk * DA:c * CW + (kk + 1) * DA]
                            for t in range(TT):
                                a = k * T + t * P
                                mm = passes(bank[4 + t][:], h_hi[:, a:a + P], h_lo[:, a:a + P], wh, wl, k == 0, k == KD - 1)
                        mm.then_inc(w_used, 1)

                    def projection(n, bk):
                        pe.wait_ge(w_ready, n + 1)
                        for k in range(KD):
                            mm = passes(bank[bk][:], *w_block(n % RING, k), *act_tile(h_hi, h_lo, k), k == 0, k == KD - 1)
                        mm.then_inc(w_used, 1)

                    def qk_stats(u):
                        g = 8 * mx + u
                        pe.wait_ge(qsq_done, g + 1)
                        pe.wait_ge(qvar_done, g) if g else None
                        pe.wait_ge(v_done, TT * (mx + 1)) if u == 0 else None
                        for t in range(TT):
                            mm = nc.tensor.matmul(bank[4][:, 2 * t:2 * t + 2], qsq[:, t * P:(t + 1) * P], one2[:, 1:3],
                                                  start=True, stop=True)
                        mm.then_inc(qst_mm, 1)

                    def qk_spread(u):
                        g = 8 * mx + u
                        pe.wait_ge(qrow_done, g + 1)
                        pe.wait_ge(qr_done, g) if g else None
                        for t in range(TT):
                            mm = nc.tensor.transpose(bank[5][:, t * P:(t + 1) * P], qrow[:, t * P:(t + 1) * P], ident[:])
                        mm.then_inc(qbc_done, 1)

                    pe.wait_ge(x_done, CREDIT + KD * p)
                    for u in range(8):
                        if u >= 4:
                            pe.wait_ge(qk_done, 8 * mx + u - 3)
                        projection(b + MIX_QK + u, u % 4)
                        if u == 0:
                            pe.wait_ge(v_done, TT * (mx + 1))
                            norm_stats(nrm)
                        if u == 1:
                            norm_spread(nrm)
                        if u >= 1:
                            qk_stats(u - 1)
                        if u >= 2:
                            qk_spread(u - 2)
                    for c in range(12):
                        bk = c % 4
                        if c < 4:
                            pe.wait_ge(qk_done, 8 * mx + 5 + c)
                        elif c < 8:
                            pe.wait_ge(cg_done, KA * mx + c - 3)
                        else:
                            pe.wait_ge(cv_chain, 4 * (KA * mx + c - 8) + 1)
                        projection(b + MIX_CONV + c, bk)
                        if c == 0:
                            qk_stats(7)
                            qk_spread(6)
                        if c == 1:
                            qk_spread(7)

                    def score_mm(s):
                        qt, h = s // HEADS, s % HEADS
                        g = UNITS * mx + s
                        qg_ = TT * mx + qt
                        nb = min(NBAND, qg_ + 1)
                        r0 = (h % 2) * HD
                        if h == 0:
                            pe.wait_ge(qrev_done, qg_ + 1)
                        if s >= 2:
                            pe.wait_ge(s_done, g - 1)
                        lhs = q_rev[qt % 2][r0:r0 + HD, (h // 2) * P:(h // 2 + 1) * P]
                        c0 = (h // 2) * S + (qg_ + 1 - nb) * P
                        for a in range(0, nb * P, 512):
                            w = min(512, nb * P - a)
                            mm = nc.tensor.matmul(spair(s)[:, a:a + w], lhs, k_sb[r0:r0 + HD, c0 + a:c0 + a + w],
                                                  start=True, stop=True)
                        mm.then_inc(s_mm, 1)

                    def prob_mm(s):
                        qt = s // HEADS
                        g = UNITS * mx + s
                        nb = min(NBAND, TT * mx + qt + 1)
                        pe.wait_ge(p_done, g + 1)
                        pe.wait_ge(pt_done, g) if g else None
                        for a in range(nb):
                            off = (s % 2) * BANDW + a * P
                            mm = nc.tensor.transpose(tpair[:, a * P:(a + 1) * P], s_sb[:, off:off + P], ident[:])
                        mm.then_inc(t_mm, 1)

                    def value_mm(s):
                        qt, h = s // HEADS, s % HEADS
                        qg_ = TT * mx + qt
                        g = UNITS * mx + s
                        nb = min(NBAND, qg_ + 1)
                        pe.wait_ge(pt_done, g + 1)
                        if h == 0 and qt >= 2:
                            pe.wait_ge(ya_ready, qg_ - 1)
                        for a in range(nb):
                            off = (s % 2) * BANDW + a * P
                            kt = qg_ + 1 - nb + a
                            mm = nc.tensor.matmul(bank[6 + qt % 2][:, h * HD:(h + 1) * HD], pT[:, off:off + P],
                                                  v_sb[:, kt * DA + h * HD:kt * DA + (h + 1) * HD],
                                                  start=(a == 0), stop=(a == nb - 1))
                        mm.then_inc(pv_mm, 1)

                    def y_turn(qt):
                        n = TT * mx + qt
                        pe.wait_ge(yn_done, n + 1)
                        for t in range(KA):
                            mm = nc.tensor.transpose(bank[6 + qt % 2][:, t * P:(t + 1) * P], ytok[:, t * P:(t + 1) * P], ident[:])
                        mm.then_inc(yT_mm, 1)

                    norm_stats(NORM_CONV[p])
                    pe.wait_ge(cv_chain, 4 * KA * (mx + 1))
                    pe.wait_ge(yc_done, KA * (mx + 1))
                    norm_spread(NORM_CONV[p])
                    pe.wait_ge(rstd_done, NORM_CONV[p] + 1)
                    for s in range(UNITS + 3):
                        if s < UNITS:
                            score_mm(s)
                        if 2 <= s < UNITS + 2:
                            prob_mm(s - 2)
                        if s >= 3:
                            value_mm(s - 3)
                        if s % HEADS == 6 and HEADS < s < UNITS:
                            y_turn(s // HEADS - 1)
                    y_turn(TT - 1)

                    with pe.Fori(0, 2) as i:
                        for m in range(4):
                            n = b + nin + m
                            pe.wait_ge(w_ready, n + 1 + 4 * i)
                            pe.wait_ge(yc_ready, KA * (mx + 1))
                            pe.wait_ge(x_done, CREDIT + KD * p + m - 3 + 4 * i)
                            for e, k in enumerate((4, 5, 6, 7, 0, 1, 2, 3)):
                                if e == 4:
                                    pe.wait_ge(ya_ready, TT * (mx + 1))
                                mm = passes(bank[m][:], *w_block(m, k), *act_tile(y_hi, y_lo, k), e == 0, e == KD - 1)
                            mm.then_inc(w_used, 1)
            norm_stats(9)
            norm_spread(9)


def kernel(**inputs):
    import numpy as np
    import concourse.bacc as bacc
    from concourse import mybir as mb
    from concourse.bass_utils import run_bass_kernel_spmd
    g = {k: np.asarray(v) for k, v in inputs.items()}

    def blocks(w):
        k, m = w.shape[0] // P, w.shape[1] // P
        return w.reshape(k, P, m, P).transpose(2, 1, 0, 3).reshape(m, P, k * P)

    def ffn_in(w):
        b = blocks(w)
        return b.reshape(2, KF, P, CW).transpose(1, 0, 2, 3).reshape(2 * KF, P, CW)

    w_in = g["w_in"][0]
    tiles = blocks(w_in)
    v = w_in[:, 2 * DA:3 * DA].reshape(4, 2, P, DA).transpose(0, 2, 1, 3).reshape(4, P, CW)
    order = [t for k in range(KA) for t in (k, KA + k)]
    order += [5 * KA + k for k in range(KA)] + [3 * KA + k for k in range(KA)] + [4 * KA + k for k in range(KA)]
    cols = lambda a: a.reshape(-1, P).T
    two = lambda a: np.concatenate([a.reshape(-1), a.reshape(-1)]).reshape(P, 1)
    arrays = {
        "xT": g["x"][0].reshape(HALVES, T, KD, P).transpose(0, 3, 2, 1).reshape(HALVES, P, KD * T),
        "w_ada": blocks(g["w_ada"][0]),
        "small": np.concatenate([cols(g["c"][0]), cols(g["b_ada"][0]), cols(g["g_norm"][0]), cols(g["g_final"][0]),
                                 two(g["q_norm_g"][0]), two(g["k_norm_g"][0]), cols(g["w_conv"][0]),
                                 cols(g["b_conv"][0]), cols(g["g_conv_out"][0])], axis=1),
        "w_f1i": ffn_in(g["w_ffn1_in"][0]), "w_f1o": blocks(g["w_ffn1_out"][0]),
        "w_mix": np.concatenate([v, tiles[order]]), "w_mo": blocks(g["w_out"][0]),
        "w_f2i": ffn_in(g["w_ffn2_in"][0]), "w_f2o": blocks(g["w_ffn2_out"][0]),
        "bias_ext": np.pad(g["rel_bias"][0][:, :2 * MAX_REL], ((0, 0), (BANDW + P - 1 - 2 * MAX_REL, 0)), mode="edge"),
        "g_attn": g["g_attn_out"][0],
    }
    nc = bacc.Bacc("TRN2", target_bir_lowering=False, num_devices=1)
    feed, args = {}, []
    for name, a in arrays.items():
        feed[name] = np.ascontiguousarray(a)
        args.append(nc.dram_tensor(name, a.shape, mb.dt.from_np(a.dtype), kind="ExternalInput").ap())
    args.append(nc.dram_tensor("out", (HALVES * KD, P, T), mb.dt.float32, kind="ExternalOutput").ap())
    build(nc, *args)
    r = run_bass_kernel_spmd(nc, [feed], core_ids=[0]).results[0]["out"]
    y = np.asarray(r).reshape(HALVES, KD, P, T).transpose(0, 3, 1, 2).reshape(1, S, D)
    return np.ascontiguousarray(y)
```

```python
from contextlib import ExitStack

import concourse.bass as bass
from concourse import mybir

F32 = mybir.dt.float32
F32R = mybir.dt.float32r
ALU = mybir.AluOpType
ACT = mybir.ActivationFunctionType

P = 128
D = 1024
S = 1024
FF = 2816
HALVES = 2
T = S // HALVES
TT = T // P
KD = D // P
KF = FF // P
DA = D // 2
KA = DA // P
HEADS = 8
HD = 64
CHUNK = 64
LEFT = 8
NBAND = LEFT * CHUNK // P + 1
BANDW = NBAND * P
MAX_REL = 128
EPS = 1e-6
NEG = -1e30

CW = KD * P
RAW = 2
RING = 4
OUT_BLOCKS = (8, 8, 6)
ADA_TILES = 3 * 3 * KD
ADA_FIRST = 20
ADA_GROUP = 4
ADA_SUMS = [(0, 4), (8, 3), (4, 4), (12, 3), (16, 4)]

PHASES = ["ffn", "ffn", "mix", "mix", "ffn", "ffn"]
IN_CHUNKS = {"ffn": 2 * KF, "mix": 24}
OUT_CHUNKS = {"ffn": 3 * KD, "mix": KD}
MIX_V, MIX_QK, MIX_CONV = 0, 4, 12
CHUNK_BASE = [sum(IN_CHUNKS[q] + OUT_CHUNKS[q] for q in PHASES[:p]) for p in range(len(PHASES))]
N_CHUNKS = sum(IN_CHUNKS[q] + OUT_CHUNKS[q] for q in PHASES)
NORM_TILES = [KD, KD, KD, KD, KA, KD, KA, KD, KD, KD]
NORM_OF_PHASE_OUT = [2, 3, 5, 7, 8, 9]
NORM_IN_PHASE = [1, 2, 3, 5, 7, 8]
NORM_CONV = {2: 4, 3: 6}

SM_C, SM_BADA, SM_GN, SM_GF, SM_QG, SM_KG, SM_WC, SM_BC, SM_GC = 0, 8, 80, 104, 112, 113, 114, 126, 130
SM_COLS = 134


def norm_sq(n):
    return sum(NORM_TILES[:n])


def norm_acc(n):
    return sum(1 + t for t in NORM_TILES[:n])


def build(nc, xT, w_ada, small, w_f1i, w_f1o, w_mix, w_mo, w_f2i, w_f2o, bias_ext, g_attn, out):
    base = (nc.sbuf_base + 31) // 32 * 32
    top = [0]

    def at(name, cols, dt, off):
        top[0] = max(top[0], off + cols * 4)
        return nc.alloc_sbuf_tensor_at(name, [P, cols], dt, offset=base + off)

    KB = 1024
    x = at("x", HALVES * KD * T, F32, 0)
    R_H = 32 * KB
    h_hi = at("h_hi", KD * T, F32R, R_H)
    h_lo = at("h_lo", KD * T, F32R, R_H + 16 * KB)
    R_HID = 64 * KB
    hid_hi = at("hid_hi", KF * T, F32R, R_HID)
    hid_lo = at("hid_lo", KF * T, F32R, R_HID + 44 * KB)
    R_W = 152 * KB
    raw = at("raw", RAW * CW, F32, R_W)
    w_hi = at("w_hi", RING * CW, F32R, R_W + 8 * KB)
    w_lo = at("w_lo", RING * CW, F32R, R_W + 24 * KB)
    R_T = 192 * KB
    sq = at("sq", T, F32, R_T)
    tmp = at("tmp", T, F32, R_T + 2 * KB)
    acc = at("acc", T, F32, R_T + 4 * KB)
    rstd = at("rstd", HALVES * T, F32, R_T + 6 * KB)
    ada_w = at("ada_w", CW, F32, R_T + 10 * KB)
    qsq = at("qsq", T, F32, R_T + 10 * KB)
    qrow = at("qrow", T, F32, R_T + 12 * KB)
    R_S = R_T + 14 * KB
    ident = at("ident", P, F32, R_S)
    sm = at("sm", SM_COLS, F32, R_S + 512)
    o = R_S + 512 + 544

    def tiny(name, cols):
        nonlocal o
        t = at(name, cols, F32, o)
        o += (cols * 4 + 31) // 32 * 32
        return t

    shift = tiny("shift", 3 * KD)
    a_scale = tiny("a_scale", 3 * KD)
    gate = tiny("gate", 3 * KD)
    s_c = tiny("s_c", KD)
    var = tiny("var", 8)
    rinv = tiny("rinv", 8)
    mhalf = tiny("mhalf", 8)
    one2 = tiny("one2", 3)
    nmax = tiny("nmax", 2)
    rsum = tiny("rsum", 2 * HEADS)
    rrec = tiny("rrec", HEADS)
    ssum = tiny("ssum", 1)
    yvar = tiny("yvar", 1)
    yr = tiny("yr", 1)
    qg = tiny("qg", 1)
    assert base + top[0] <= nc.sbuf_usable_end, (base + top[0], nc.sbuf_usable_end)

    ada0 = at("ada0", ADA_FIRST * CW, F32, R_HID)
    ada_acc = at("ada_acc", ADA_GROUP * P, F32, R_HID + 80 * KB)
    ada_acc2 = at("ada_acc2", 6 * P, F32, R_H + 28 * KB)
    START = 3
    start_ring = at("start_ring", START * T, F32, R_HID + 82 * KB)
    q_sb = at("q_sb", KA * T, F32, R_HID)
    k_sb = at("k_sb", KA * S, F32, R_HID + 8 * KB)
    v_sb = at("v_sb", (S // P) * DA, F32, R_HID + 24 * KB)
    yc = at("yc", KA * T, F32, R_HID + 40 * KB)
    y_hi = at("y_hi", KD * T, F32R, R_HID + 48 * KB)
    y_lo = at("y_lo", KD * T, F32R, R_HID + 64 * KB)
    cg = at("cg", KA * T, F32, R_HID + 48 * KB)
    UW = T + 2
    u_sb = at("u_sb", KA * UW, F32, R_HID + 56 * KB)
    ytok = at("ytok", DA, F32, R_HID + 80 * KB)
    g_row = at("g_row", DA, F32, R_HID + 82 * KB)
    halo = at("halo", KA * 2, F32, R_HID + 84 * KB)
    q_rev1 = at("q_rev1", KA * P, F32, R_HID + 84 * KB + 64)
    bias = at("bias", HEADS * BANDW, F32, R_H)
    s_sb = at("s_sb", 2 * BANDW, F32, R_H + 20 * KB)
    pT = at("pT", 2 * BANDW, F32, R_H + 25 * KB)
    q_rev0 = at("q_rev0", KA * P, F32, R_H + 30 * KB)
    q_rev = [q_rev1, q_rev0]
    out_sb = at("out_sb", KD * T, F32, R_H)
    out_sb1 = at("out_sb1", KD * T, F32, R_H + 16 * KB)

    def col(t, start, n):
        return t[:, bass.ds(start, n)]

    ctx = ExitStack()
    with ctx:
        pair = [ctx.enter_context(nc.psum_tensor(f"pair{i}", [P, 1024], F32)) for i in range(4)]
        bank = [pair[i // 2][:, (i % 2) * 512:(i % 2 + 1) * 512] for i in range(8)]
        tpair = pair[2]
        STAT, ADAB = 6, 7
        GATE_B = (4, 5, 6, 7)

        def y_bank(qt):
            return bank[7 - qt % 2]

        def sem(name):
            return ctx.enter_context(nc.semaphore(name))

        small_in = sem("small_in")
        x_in = [[sem("x_in0a"), sem("x_in0b")], [sem("x_in1")]]
        ada0_in = [sem(f"ada0_in{g}") for g in range(ADA_FIRST // ADA_GROUP)]
        raw_in = [sem(f"raw_in{i}") for i in range(RAW)]
        w_hi_done = sem("w_hi_done")
        w_ready = sem("w_ready")
        w_used = sem("w_used")
        gate_done = sem("gate_done")
        prod_done = sem("prod_done")
        hid_hi_done = sem("hid_hi_done")
        hid_done = sem("hid_done")
        x_done = sem("x_done")
        h_tmp = sem("h_tmp")
        h_hi_done = sem("h_hi_done")
        h_ready = sem("h_ready")
        sq_done = sem("sq_done")
        acc_done = sem("acc_done")
        stat_mm = sem("stat_mm")
        var_done = sem("var_done")
        pow_done = sem("pow_done")
        bc_done = sem("bc_done")
        rstd_done = sem("rstd_done")
        const_done = sem("const_done")
        sc_done = sem("sc_done")
        ada_chain = sem("ada_chain")
        ada_in = sem("ada_in")
        ada_pool = sem("ada_pool")
        ada_ready = sem("ada_ready")
        ada_mm = sem("ada_mm")
        ada_rest_mm = sem("ada_rest_mm")
        h_free = sem("h_free")
        mod_chain = sem("mod_chain")
        v_done = sem("v_done")
        qsq_done = sem("qsq_done")
        qst_mm = sem("qst_mm")
        qvar_done = sem("qvar_done")
        qpow_done = sem("qpow_done")
        qrow_done = sem("qrow_done")
        qbc_done = sem("qbc_done")
        qr_done = sem("qr_done")
        qk_done = sem("qk_done")
        cg_done = sem("cg_done")
        u_done = sem("u_done")
        cv_chain = sem("cv_chain")
        yc_done = sem("yc_done")
        halo_done = sem("halo_done")
        y_tmp = sem("y_tmp")
        y_hi_done = sem("y_hi_done")
        yc_ready = sem("yc_ready")
        grow_in = sem("grow_in")
        bias_in = [sem(f"bias_in{h}") for h in range(HEADS)]
        bias_ok = sem("bias_ok")
        qrev_done = sem("qrev_done")
        s_mm = sem("s_mm")
        s_done = sem("s_done")
        p_done = sem("p_done")
        t_mm = sem("t_mm")
        pt_done = sem("pt_done")
        pv_mm = sem("pv_mm")
        rrec_done = sem("rrec_done")
        yt_done = sem("yt_done")
        ysq_done = sem("ysq_done")
        yvar_done = sem("yvar_done")
        ypow_done = sem("ypow_done")
        yn_done = sem("yn_done")
        yT_mm = sem("yT_mm")
        ya_hi_done = sem("ya_hi_done")
        ya_ready = sem("ya_ready")
        out_done = sem("out_done")
        out_stored = sem("out_stored")
        CREDIT = 4

        block = ctx.enter_context(nc.Block())

        def wc(tap, ct):
            return sm[:, SM_WC + tap * KA + ct:SM_WC + tap * KA + ct + 1]

        def ph(p):
            return CHUNK_BASE[p], IN_CHUNKS[PHASES[p]], PHASES[p]

        J_BASE = {0: 0, 1: KF, 4: 2 * KF, 5: 3 * KF}
        ADA_IN_BASE = {0: ADA_FIRST, 1: ADA_FIRST + KF + KD}
        ADA_OUT_BASE = {0: ADA_FIRST + KF}
        MIX_NO = {2: 0, 3: 1}
        UNITS = TT * HEADS
        CONV_SQUARE, CONV_STATS, CONV_SPREAD = 2, 8, 10
        CONV_SPLIT = [(12, 14, 15, 17), (17, 20, 25, 28)]
        OUT_SPLITS = (3, 4, 9, 12)
        H_EARLY = 5
        OUT_EARLY = {20: 1, 26: 3}

        def tile_at(mx, i):
            return TT - 1 - i if mx == 0 else i

        def key_tiles(mx, i):
            return min(NBAND, TT * mx + tile_at(mx, i) + 1)

        def spair(s):
            return pair[s % 2]

        def mod_col(sub, part, k):
            return (3 * sub + part) * KD + k

        @block.sync
        def _(sp):
            sp.dma_start(sm[:], small).then_inc(small_in, 16)

            def ada_load(g):
                src = w_ada[bass.ds(g * ADA_GROUP, ADA_GROUP)].rearrange("a p c -> p a c")
                dst = col(ada0, g * ADA_GROUP * CW, ADA_GROUP * CW).rearrange("p (a c) -> p a c", a=ADA_GROUP)
                sp.dma_start(dst, src).then_inc(ada0_in[g], 16)

            def load(n, src, cols, slot):
                if not (isinstance(n, int) and n < RAW):
                    sp.wait_ge(w_ready, n - RAW + 1)
                sp.dma_start(col(raw, slot * CW, cols), src).then_inc(raw_in[slot], 16)

            def chunk_src(w, i):
                return w[bass.ds(i, 1)].rearrange("a p c -> (a p) c")

            HX = KD * T // 2
            for e in range(2):
                sp.dma_start(col(x, e * HX, HX), xT[0, :, e * HX:(e + 1) * HX]).then_inc(x_in[0][e], 16)
            ada_load(0)
            ada_load(2)
            for c in range(RAW):
                load(c, chunk_src(w_f1i, c), CW, c)
            ada_load(1)
            ada_load(3)
            for c in range(RAW, 4):
                load(c, chunk_src(w_f1i, c), CW, c % RAW)
            sp.dma_start(col(x, KD * T, KD * T), xT[1]).then_inc(x_in[1][0], 16)
            ada_load(4)
            for p in range(len(PHASES)):
                b, nin, kind = ph(p)
                win = {"ffn": w_f1i if p < 2 else w_f2i, "mix": w_mix}[kind]
                wout = {"ffn": w_f1o if p < 2 else w_f2o, "mix": w_mo}[kind]
                with sp.Fori(1 if p == 0 else 0, nin // 4) as i:
                    for c in range(4):
                        load(b + 4 * i + c, chunk_src(win, 4 * i + c), CW, c % RAW)
                if kind == "ffn":
                    with sp.Fori(0, 2) as i:
                        for m in range(4):
                            for c, nb in enumerate(OUT_BLOCKS):
                                e = 3 * m + c
                                src = wout[bass.ds(4 * i + m, 1), :, c * CW:c * CW + nb * P].rearrange("a p c -> (a p) c")
                                load(b + nin + 12 * i + e, src, nb * P, e % RAW)
                else:
                    def bias_load(h):
                        last = min(((h + 1) * BANDW - 1) // T, KD - 1)
                        if last < KD - 1:
                            sp.wait_ge(h_free, (KD - 1) * MIX_NO[p] + last + 1)
                        else:
                            sp.wait_ge(w_used, b + MIX_CONV + 12)
                        src = bass.AP(bias_ext.tensor, h * (BANDW + P - 1), [[1, P], [1, BANDW]])
                        sp.dma_start(col(bias, h * BANDW, BANDW), src).then_inc(bias_in[h], 16)

                    def out_load(i, m):
                        load(b + nin + 4 * i + m, chunk_src(wout, 4 * i + m), CW, m % RAW)

                    if p == 2:
                        g0 = bass.AP(g_attn.tensor, 0, [[0, P], [1, DA]])
                        sp.dma_start(g_row[:], g0).then_inc(grow_in, 16)
                    for h in range(5):
                        bias_load(h)
                    for m in range(RAW):
                        out_load(0, m)
                    for h in range(5, HEADS):
                        bias_load(h)
                    for m in range(RAW, 4):
                        out_load(0, m)
                    with sp.Fori(1, 2) as i:
                        for m in range(4):
                            out_load(i, m)

        @block.gpsimd
        def _(pool):
            nc.gpsimd.memset(ident[:], 0.0).then_inc(const_done, 1)
            nc.gpsimd.memset(mhalf[:], -0.5).then_inc(const_done, 1)
            nc.gpsimd.memset(one2[:], 1.0).then_inc(const_done, 1)
            pool.wait_ge(const_done, 3)
            nc.gpsimd.affine_select(out=ident[:], in_=ident[:], compare_op=ALU.not_equal, fill=1.0, base=0,
                                    pattern=[[-1, P]], channel_multiplier=1).then_inc(const_done, 1)
            pool.wait_ge(const_done, 4)
            nc.gpsimd.memset(one2[64:128, 1:2], 0.0).then_inc(const_done, 1)
            pool.wait_ge(const_done, 5)
            nc.gpsimd.memset(one2[0:64, 2:3], 0.0).then_inc(const_done, 1)

            def power(n):
                pool.wait_ge(var_done, n + 1)
                pool.wait_ge(bc_done, n) if n else None
                nc.gpsimd.tensor_tensor(rinv[:, 0:TT], var[:, 0:TT], mhalf[:, 0:TT], ALU.pow).then_inc(pow_done, 1)

            def ada_tile(f, k):
                if not isinstance(k, int):
                    pool.wait_ge(ada_mm, f - ADA_GROUP)
                elif k:
                    pool.wait_ge(ada_mm, 9)
                src = w_ada[bass.ds(f, 1)].rearrange("a p c -> (a p) c")
                pool.dma_start(ada_w[:], src).then_inc(ada_in, 16)
                pool.wait_ge(ada_in, 16 * k + 16)
                w3 = ada_w[:].rearrange("p (k c) -> p k c", k=KD)
                sc = bass.AP(s_c[:].tensor, s_c[:].offset, [list(s_c[:].ap[0]), [1, KD], [0, P]])
                nc.gpsimd.tensor_tensor(w3, w3, sc, ALU.mult).then_inc(ada_pool, 1)
                for e, w in enumerate((512, 256)):
                    pool.wait_ge(ada_pool, 3 * k + e + 1)
                    nc.gpsimd.tensor_tensor(ada_w[:, 0:w], ada_w[:, 0:w], ada_w[:, w:2 * w], ALU.add).then_inc(ada_pool, 1)
                pool.wait_ge(ada_pool, 3 * k + 3)
                nc.gpsimd.tensor_tensor(ada_w[:, 0:128], ada_w[:, 0:128], ada_w[:, 128:256], ALU.add).then_inc(ada_ready, 1)

            pool.wait_ge(const_done, 6)
            pool.wait_ge(sc_done, 1)
            power(0)
            for p in range(len(PHASES)):
                b, nin, kind = ph(p)
                if p in ADA_IN_BASE:
                    f0 = ADA_IN_BASE[p]
                    if p == 0:
                        ada_tile(f0, 0)
                        ada_tile(f0 + 1, 1)
                    with pool.Fori(2 if p == 0 else 0, KF - 2) as j:
                        ada_tile(f0 + j, f0 - ADA_FIRST + j)
                    power(NORM_IN_PHASE[p])
                    with pool.Fori(KF - 2, KF) as j:
                        ada_tile(f0 + j, f0 - ADA_FIRST + j)
                if p in ADA_OUT_BASE:
                    f0 = ADA_OUT_BASE[p]
                    with pool.Fori(0, KD) as j:
                        ada_tile(f0 + j, f0 - ADA_FIRST + j)
                if kind == "ffn" and p > 1:
                    power(NORM_IN_PHASE[p])
                if kind == "mix":
                    mx = MIX_NO[p]
                    power(NORM_IN_PHASE[p])
                    for u in range(8):
                        g = 8 * mx + u
                        pool.wait_ge(qvar_done, g + 1)
                        pool.wait_ge(qbc_done, g) if g else None
                        pool.wait_ge(bc_done, NORM_IN_PHASE[p] + 1) if u == 0 else None
                        nc.gpsimd.tensor_tensor(rinv[:], var[:], mhalf[:], ALU.pow).then_inc(qpow_done, 1)
                        pool.wait_ge(qpow_done, g + 1)
                        wide = bass.AP(rinv[:].tensor, rinv[:].offset, [list(rinv[:].ap[0]), [1, 2 * TT], [0, HD]])
                        nc.gpsimd.tensor_copy(qrow[:].rearrange("p (r d) -> p r d", d=HD), wide).then_inc(qrow_done, 1)
                    def reverse_q(qt):
                        n = TT * mx + qt
                        if qt == 0:
                            pool.wait_ge(qk_done, 8 * (mx + 1))
                        if qt >= 2:
                            pool.wait_ge(s_mm, UNITS * mx + HEADS * (qt - 1))
                        src = bass.AP(q_sb[:].tensor, q_sb[:].offset + tile_at(mx, qt) * P + P - 1,
                                      [list(q_sb[:].ap[0]), [T, KA], [-1, P]])
                        nc.gpsimd.tensor_copy(q_rev[qt % 2][:].rearrange("p (t c) -> p t c", t=KA), src)\
                            .then_inc(qrev_done, 1)
                    reverse_q(0)
                    for h in range(HEADS):
                        pool.wait_ge(bias_in[h], 16 * (mx + 1))
                        if h:
                            pool.wait_ge(bias_ok, 2 * (HEADS * mx + h))
                        else:
                            pool.wait_ge(qrev_done, TT * mx + 1)
                        nc.gpsimd.memset(bias[64:128, h * BANDW + BANDW - 64:h * BANDW + BANDW], NEG).then_inc(bias_ok, 1)
                        pool.wait_ge(bias_ok, 2 * (HEADS * mx + h) + 1)
                        nc.gpsimd.memset(bias[0:64, h * BANDW:h * BANDW + 64], NEG).then_inc(bias_ok, 1)
                    pool.wait_ge(bias_ok, 2 * HEADS * (mx + 1))
                    reverse_q(1)
                    for m in range(4):
                        if m == 2:
                            power(NORM_CONV[p])
                        n = b + nin + m
                        pool.wait_ge(w_hi_done, n + 1)
                        sl, rs = (n % RING) * CW, (n % RAW) * CW
                        nc.gpsimd.tensor_tensor(col(w_lo, sl, CW), col(raw, rs, CW), col(w_hi, sl, CW).bitcast(F32),
                                                ALU.subtract).then_inc(w_ready, 1)
                    for qt in range(TT):
                        if 2 <= qt + 1 < TT:
                            reverse_q(qt + 1)
                        n = TT * mx + qt
                        pool.wait_ge(yvar_done, n + 1)
                        nc.gpsimd.tensor_tensor(yr[:], yvar[:], mhalf[:, 0:1], ALU.pow).then_inc(ypow_done, 1)
                    with pool.Fori(0, KD) as m:
                        n = NORM_OF_PHASE_OUT[p]
                        pool.wait_ge(sq_done, norm_sq(n) + 1 + m)
                        pool.wait_ge(acc_done, norm_acc(n) + 1 + m)
                        nc.gpsimd.tensor_tensor(acc[:], acc[:], sq[:], ALU.add).then_inc(acc_done, 1)
            power(9)

        @block.scalar
        def _(act):
            def split_hi(nb, k, c):
                n = nb + c
                slot = n % RING
                act.wait_ge(raw_in[n % RAW], 16 * (n // RAW + 1) + 8 * k)
                if not (isinstance(k, int) and n + k < RING):
                    act.wait_ge(w_used, n - RING + 1 + k)
                nc.scalar.copy(col(w_hi, slot * CW, CW), col(raw, (n % RAW) * CW, CW)).then_inc(w_hi_done, 1)

            def square(src, n, t):
                s = norm_sq(n) + t
                a = norm_acc(n) + 1 + t
                if isinstance(t, int) and t == 0 and n > 0:
                    a = norm_acc(n)
                if not (isinstance(t, int) and s == 0):
                    act.wait_ge(acc_done, a)
                nc.scalar.activation(sq[:], src, ACT.Square).then_inc(sq_done, 1)

            def spread(n, dst):
                act.wait_ge(bc_done, n + 1)
                nc.scalar.copy(dst, bank[STAT][:]).then_inc(rstd_done, 1)

            def h_part(ne, m, sub):
                act.wait_ge(h_tmp, KD * ne + m + 1)
                nc.scalar.activation(col(h_hi, m * T, T), tmp[:], ACT.Identity,
                                     bias=shift[:, bass.ds(sub * KD + m, 1)]).then_inc(h_hi_done, 1)

            def store(m):
                act.wait_ge(out_done, m + 1)
                src = col(out_sb if m < KD else out_sb1, (m % KD) * T, T)
                act.dma_start(out[m], src).then_inc(out_stored, 16)

            act.wait_ge(small_in, 16)
            nc.scalar.activation(s_c[:], sm[:, SM_C:SM_C + KD], ACT.Silu).then_inc(sc_done, 1)
            def square_first(hf, t):
                if t == 0 or (hf, t) == (0, KD // 2):
                    act.wait_ge(x_in[hf][t // (KD // 2)], 16)
                if t >= START:
                    act.wait_ge(acc_done, norm_acc(hf) + t - START + 2)
                elif hf == 1:
                    act.wait_ge(h_ready, KD)
                nc.scalar.activation(col(start_ring, (t % START) * T, T), col(x, (hf * KD + t) * T, T), ACT.Square)\
                    .then_inc(sq_done, 1)

            def h_part_first(m):
                act.wait_ge(h_tmp, m + 1)
                nc.scalar.activation(col(h_hi, m * T, T), col(start_ring, (m % START) * T, T), ACT.Identity,
                                     bias=shift[:, m:m + 1]).then_inc(h_hi_done, 1)

            for t in range(KD):
                square_first(0, t)
            spread(0, col(rstd, 0, T))
            split_hi(0, 0, 0)
            split_hi(0, 0, 1)
            for m in range(KD // 2):
                h_part_first(m)
            split_hi(0, 0, 2)
            split_hi(0, 0, 3)
            for m in range(KD // 2, KD):
                h_part_first(m)
            for t in range(KD):
                square_first(1, t)

            def ffn_in(p, i, jj):
                b, j0 = CHUNK_BASE[p], J_BASE[p]
                n, jl = b + 2 * jj, j0 + jj
                act.wait_ge(w_used, n + 1 + 4 * i)
                act.wait_ge(prod_done, CREDIT + jl + 2 * i)
                nc.scalar.activation(sq[:], bank[jj][:], ACT.Silu).then_inc(gate_done, 1)
                split_hi(b + RING, 4 * i, 2 * jj)
                split_hi(b + RING, 4 * i, 2 * jj + 1)
                act.wait_ge(prod_done, CREDIT + jl + 1 + 2 * i)
                nc.scalar.copy(col(hid_hi, (2 * i + jj) * T, T), tmp[:]).then_inc(hid_hi_done, 1)

            def side(p, m):
                if p + 1 < len(PHASES):
                    h_part(p + 1, m, (p + 1) // 2)

            def out_tile(p, i, m, last):
                b, nin, kind = ph(p)
                per = 3 if kind == "ffn" else 1
                k = 4 * per * i
                n = b + nin + per * m
                if per == 1:
                    side(p, 4 * i + m)
                for c in range(per):
                    if c == 1:
                        side(p, 4 * i + m)
                    if not (last and per * m + c >= 4 * per - RING):
                        split_hi(n + RING, k, c)
                act.wait_ge(x_done, CREDIT + KD * p + m + 1 + 4 * i)
                square(col(x, ((p % 2) * KD + m + 4 * i) * T, T), NORM_OF_PHASE_OUT[p], 4 * i + m)
                if p + 1 == len(PHASES):
                    store(4 * i + m)

            for p in range(len(PHASES)):
                b, nin, kind = ph(p)
                nrm = NORM_IN_PHASE[p]
                if kind == "ffn":
                    act.wait_ge(acc_done, norm_acc(nrm) + 1 + NORM_TILES[nrm])
                    with act.Fori(0, KF // 2 - 1) as i:
                        for jj in range(2):
                            ffn_in(p, i, jj)
                    for jj in range(2):
                        ffn_in(p, KF // 2 - 1, jj)
                    spread(nrm, col(rstd, ((p + 1) % 2) * T, T))
                else:
                    mx = MIX_NO[p]
                    for c in range(4):
                        split_hi(b + RING, 0, c)
                    for t in range(TT):
                        act.wait_ge(w_used, b + MIX_QK)
                        nc.scalar.copy(col(v_sb, (TT * mx + t) * DA, DA), bank[4 + t][:]).then_inc(v_done, 1)

                    def qk_square(u):
                        g = 8 * mx + u
                        act.wait_ge(w_used, b + MIX_QK + u + 1)
                        act.wait_ge(qst_mm, g) if g else None
                        nc.scalar.activation(qsq[:], bank[u % 4][:], ACT.Square).then_inc(qsq_done, 1)

                    def qk_spread(u):
                        g = 8 * mx + u
                        act.wait_ge(qbc_done, g + 1)
                        act.wait_ge(qk_done, g) if g else None
                        nc.scalar.copy(sq[:], bank[5][:]).then_inc(qr_done, 1)

                    for u in range(8):
                        qk_square(u)
                        split_hi(b + RING + MIX_QK, 0, u)
                        if u == 1:
                            spread(nrm, col(rstd, ((p + 1) % 2) * T, T))
                        if u >= 2:
                            qk_spread(u - 2)
                    for c in range(12):
                        if c < 4:
                            act.wait_ge(w_used, b + MIX_CONV + c + 1)
                            nc.scalar.copy(col(cg, c * T, T), bank[c][:]).then_inc(cg_done, 1)
                            if c < 2:
                                qk_spread(6 + c)
                        if c < 8:
                            split_hi(b + RING + MIX_CONV, 0, c)

                    def conv_square(ct):
                        act.wait_ge(yc_done, KA * mx + ct + 1)
                        square(col(yc, ct * T, T), NORM_CONV[p], ct)

                    def conv_part(ct):
                        act.wait_ge(y_tmp, KA * mx + ct + 1)
                        nc.scalar.copy(col(y_hi, (KA + ct) * T, T), tmp[:]).then_inc(y_hi_done, 1)

                    def softmax(s):
                        qt, h = s // HEADS, s % HEADS
                        nb = key_tiles(mx, qt)
                        g = UNITS * mx + s
                        act.wait_ge(s_done, g + 1)
                        if h == 0 and TT * mx + qt >= 2:
                            act.wait_ge(rrec_done, TT * mx + qt - 1)
                        sl = s_sb[:, (s % 2) * BANDW:(s % 2) * BANDW + nb * P]
                        r = (qt % 2) * HEADS + h
                        nc.scalar.activation(sl, sl, ACT.Exp, scale=-1.0, bias=nmax[:, s % 2:s % 2 + 1],
                                             accum_out=rsum[:, r:r + 1]).then_inc(p_done, 1)

                    def y_square(qt):
                        n = TT * mx + qt
                        act.wait_ge(yt_done, n + 1)
                        act.wait_ge(yvar_done, n) if n else None
                        nc.scalar.activation(sq[:], ytok[:], ACT.Square, accum_out=ssum[:]).then_inc(ysq_done, 1)

                    def y_split(qt):
                        n = TT * mx + qt
                        act.wait_ge(yT_mm, n + 1)
                        yb = y_bank(qt)
                        src = bass.AP(yb[:].tensor, yb[:].offset + P - 1, [list(yb[:].ap[0]), [P, KA], [-1, P]])
                        c = tile_at(mx, qt) * P
                        dst = y_hi[:, 0:KA * T].rearrange("p (t c) -> p t c", t=KA)[:, :, c:c + P]
                        nc.scalar.copy(dst, src).then_inc(ya_hi_done, 1)

                    for s in range(UNITS):
                        softmax(s)
                        if 0 <= s - CONV_SQUARE < KA:
                            conv_square(s - CONV_SQUARE)
                        if s in OUT_SPLITS:
                            split_hi(b + RING + MIX_CONV, 0, 8 + OUT_SPLITS.index(s))
                        if s == CONV_SPREAD:
                            spread(NORM_CONV[p], col(rstd, (p % 2) * T, T))
                        if s in CONV_SPLIT[mx]:
                            conv_part(CONV_SPLIT[mx].index(s))
                        if s % HEADS == 4 and s > HEADS:
                            y_square(s // HEADS - 1)
                        if s % HEADS == 0 and s > HEADS:
                            y_split(s // HEADS - 2)
                    y_split(TT - 2)
                    y_square(TT - 1)
                    y_split(TT - 1)
                if p + 1 < len(PHASES):
                    with act.Fori(0, 2) as i:
                        for m in range(4):
                            out_tile(p, i, m, False)
                else:
                    for i in range(2):
                        for m in range(4):
                            out_tile(p, i, m, i == 1)
            spread(9, col(rstd, T, T))
            for m in range(KD, HALVES * KD):
                store(m)
            act.wait_ge(out_stored, 16 * HALVES * KD)

        @block.vector
        def _(dve):
            nc.vector.memset(var[:], 0.0).then_inc(gate_done, CREDIT)
            nc.vector.memset(nmax[:], 0.0).then_inc(prod_done, CREDIT)
            nc.vector.memset(yvar[:], 0.0).then_inc(x_done, CREDIT)
            nc.vector.memset(rrec[:], 0.0).then_inc(hid_done, CREDIT)
            nc.vector.memset(acc[:], 0.0).then_inc(acc_done, 1)

            def split_lo(nb, k, c):
                n = nb + c
                slot = n % RING
                dve.wait_ge(w_hi_done, n + 1 + k)
                nc.vector.tensor_tensor(col(w_lo, slot * CW, CW), col(raw, (n % RAW) * CW, CW),
                                        col(w_hi, slot * CW, CW).bitcast(F32), ALU.subtract).then_inc(w_ready, 1)

            def add_square(n, t):
                dve.wait_ge(sq_done, norm_sq(n) + t + 1)
                dve.wait_ge(acc_done, norm_acc(n) + t + 1)
                nc.vector.tensor_tensor(acc[:], acc[:], sq[:], ALU.add).then_inc(acc_done, 1)

            def mean(n):
                width = NORM_TILES[n] * P
                dve.wait_ge(stat_mm, n + 1)
                if n:
                    dve.wait_ge(pow_done, n)
                if n in (4, 6):
                    dve.wait_ge(qpow_done, 4 * n - 8)
                nc.vector.tensor_scalar(var[:, 0:TT], bank[STAT][:, 0:TT], 1.0 / width, EPS,
                                        ALU.mult, ALU.add).then_inc(var_done, 1)
                if n < 9:
                    nc.vector.memset(acc[:], 0.0).then_inc(acc_done, 1)

            def h_first(ne, m, sub, hf):
                g = KD * ne + m
                if not (isinstance(m, int) and g == 0):
                    dve.wait_ge(h_ready, g)
                nc.vector.scalar_tensor_tensor(tmp[:], col(x, (hf * KD + m) * T, T),
                                               a_scale[:, bass.ds(sub * KD + m, 1)], col(rstd, hf * T, T),
                                               ALU.mult, ALU.mult).then_inc(h_tmp, 1)

            def h_second(ne, m, sub):
                dve.wait_ge(h_hi_done, KD * ne + m + 1)
                nc.vector.scalar_tensor_tensor(col(h_lo, m * T, T), tmp[:], shift[:, bass.ds(sub * KD + m, 1)],
                                               col(h_hi, m * T, T).bitcast(F32), ALU.add, ALU.subtract)\
                    .then_inc(h_ready, 1)

            chain = [0]

            def link(ins):
                chain[0] += 1
                ins.then_inc(mod_chain, 1)
                dve.wait_ge(mod_chain, chain[0])

            def modulation(sub, parts, k0=0, k1=KD):
                lo, hi = sub * KD + k0, sub * KD + k1
                for part in parts:
                    f, e = mod_col(sub, part, k0), mod_col(sub, part, k1)
                    src, b_ = bank[ADAB][:, f:e], sm[:, SM_BADA + f:SM_BADA + e]
                    if part == 0:
                        link(nc.vector.tensor_tensor(shift[:, lo:hi], src, b_, ALU.add))
                    if part == 1:
                        d = a_scale[:, lo:hi]
                        link(nc.vector.tensor_tensor(d, src, b_, ALU.add))
                        link(nc.vector.scalar_tensor_tensor(d, d, 1.0, sm[:, SM_GN + lo:SM_GN + hi],
                                                            ALU.add, ALU.mult))
                    if part == 2:
                        d = gate[:, lo:hi]
                        link(nc.vector.tensor_tensor(d, src, b_, ALU.add))
                        w = 1.0 if sub == 1 else 0.5
                        link(nc.vector.tensor_scalar(d, d, 1.0, w, ALU.add, ALU.mult))

            dve.wait_ge(sc_done, 1)
            nc.vector.tensor_scalar(qg[:], sm[:, SM_QG:SM_QG + 1], HD ** -0.5, None, ALU.mult)

            def ada_first(n, k0, k1):
                f, tiles = ADA_SUMS[n]
                if k0 == 0:
                    dve.wait_ge(ada0_in[f // ADA_GROUP], 16)
                    if n == 2:
                        dve.wait_ge(ada_mm, 8)
                    if n == 4:
                        dve.wait_ge(ada_mm, 17)
                w4 = col(ada0, f * CW, tiles * CW).rearrange("p (a k c) -> p a k c", a=tiles, k=KD)
                dst = {1: col(ada_acc2, 0, 3 * P), 3: col(ada_acc2, 3 * P, 3 * P)}.get(n, ada_acc[:])
                a3 = dst.rearrange("p (a c) -> p a c", a=tiles)
                for k in range(k0, k1):
                    if k == 0:
                        nc.vector.tensor_scalar(a3, w4[:, :, 0, :], s_c[:, 0:1], None, ALU.mult).then_inc(ada_chain, 1)
                    else:
                        dve.wait_ge(ada_chain, KD * n + k)
                        nc.vector.scalar_tensor_tensor(a3, w4[:, :, k, :], s_c[:, k:k + 1], a3,
                                                       ALU.mult, ALU.add).then_inc(ada_chain, 1)

            def add_first(hf, t):
                dve.wait_ge(sq_done, norm_sq(hf) + t + 1)
                dve.wait_ge(acc_done, norm_acc(hf) + t + 1)
                nc.vector.tensor_tensor(acc[:], acc[:], col(start_ring, (t % START) * T, T), ALU.add).then_inc(acc_done, 1)

            def h_some(m0, m1):
                for m in range(m0, m1 + 1):
                    slot = col(start_ring, (m % START) * T, T)
                    if m < m1:
                        if m >= START:
                            dve.wait_ge(h_ready, m - START + 1)
                        nc.vector.scalar_tensor_tensor(slot, col(x, m * T, T), a_scale[:, m:m + 1], col(rstd, 0, T),
                                                       ALU.mult, ALU.mult).then_inc(h_tmp, 1)
                    if m > m0:
                        slot = col(start_ring, ((m - 1) % START) * T, T)
                        dve.wait_ge(h_hi_done, m)
                        nc.vector.scalar_tensor_tensor(col(h_lo, (m - 1) * T, T), slot, shift[:, m - 1:m],
                                                       col(h_hi, (m - 1) * T, T).bitcast(F32), ALU.add, ALU.subtract)\
                            .then_inc(h_ready, 1)

            for t in range(KD):
                add_first(0, t)
            ada_first(0, 0, 3)
            mean(0)
            ada_first(0, 3, KD)
            ada_first(1, 0, KD)
            split_lo(0, 0, 0)
            split_lo(0, 0, 1)
            dve.wait_ge(ada_mm, 8)
            modulation(0, (0, 1), 0, KD // 2)
            dve.wait_ge(rstd_done, 1)
            h_some(0, KD // 2)
            ada_first(2, 0, KD)
            ada_first(3, 0, KD)
            split_lo(0, 0, 2)
            dve.wait_ge(ada_mm, 17)
            modulation(0, (0, 1), KD // 2, KD)
            split_lo(0, 0, 3)
            h_some(KD // 2, KD)
            for t in range(KD):
                add_first(1, t)

            def ffn_in(p, i, jj):
                b, j0 = CHUNK_BASE[p], J_BASE[p]
                jl = j0 + jj
                split_lo(b + RING, 4 * i, 2 * jj)
                dve.wait_ge(gate_done, CREDIT + jl + 1 + 2 * i)
                dve.wait_ge(w_used, b + 2 * jj + 2 + 4 * i)
                dve.wait_ge(hid_done, CREDIT + jl + 2 * i)
                nc.vector.tensor_tensor(tmp[:], sq[:], bank[2 + jj][:], ALU.mult).then_inc(prod_done, 1)
                split_lo(b + RING, 4 * i, 2 * jj + 1)
                dve.wait_ge(hid_hi_done, jl + 1 + 2 * i)
                hj = (2 * i + jj) * T
                nc.vector.tensor_tensor(col(hid_lo, hj, T), tmp[:], col(hid_hi, hj, T).bitcast(F32), ALU.subtract)\
                    .then_inc(hid_done, 1)

            def side_first(p, m):
                if p + 1 < len(PHASES):
                    h_first(p + 1, m, (p + 1) // 2, (p + 1) % 2)

            def side_second(p, m):
                if p + 1 < len(PHASES):
                    h_second(p + 1, m, (p + 1) // 2)
                else:
                    final(m, 0, out_sb)

            def final(m, hf, dst):
                nc.vector.scalar_tensor_tensor(col(dst, m * T, T), col(x, (hf * KD + m) * T, T),
                                               sm[:, SM_GF + m:SM_GF + m + 1], col(rstd, hf * T, T),
                                               ALU.mult, ALU.mult).then_inc(out_done, 1)

            def out_tile(p, i, m, last):
                b, nin, kind = ph(p)
                per = 3 if kind == "ffn" else 1
                k = 4 * per * i
                n = b + nin + per * m
                hf, sub = p % 2, p // 2

                def split_c(c):
                    if not (last and per * m + c >= 4 * per - RING):
                        split_lo(n + RING, k, c)

                if per == 3:
                    split_c(0)
                side_first(p, 4 * i + m)
                if per == 3:
                    split_c(1)
                side_second(p, 4 * i + m)
                dve.wait_ge(w_used, n + per + k)
                xt = col(x, (hf * KD + m + 4 * i) * T, T)
                nc.vector.scalar_tensor_tensor(xt, bank[m][:], gate[:, bass.ds(sub * KD + m + 4 * i, 1)], xt,
                                               ALU.mult, ALU.add).then_inc(x_done, 1)
                split_c(2 if per == 3 else 0)
                if kind == "ffn":
                    add_square(NORM_OF_PHASE_OUT[p], 4 * i + m)

            for p in range(len(PHASES)):
                b, nin, kind = ph(p)
                nrm = NORM_IN_PHASE[p]
                dve.wait_ge(h_ready, KD * (p + 1))
                if kind == "ffn":
                    if p == 0:
                        for jj in range(2):
                            ffn_in(p, 0, jj)
                        ada_first(4, 0, KD)
                    with dve.Fori(1 if p == 0 else 0, KF // 2 - 1) as i:
                        for jj in range(2):
                            ffn_in(p, i, jj)
                    mean(nrm)
                    for jj in range(2):
                        ffn_in(p, KF // 2 - 1, jj)
                    if p == 0:
                        dve.wait_ge(ada_rest_mm, ADA_GROUP)
                        dve.wait_ge(ada_mm, ADA_FIRST - ADA_GROUP + KF)
                        modulation(0, (2,))
                        modulation(1, (0, 1))
                    if p == 1:
                        dve.wait_ge(ada_mm, ADA_TILES - ADA_GROUP)
                        modulation(1, (2,))
                        modulation(2, (0, 1, 2))
                    dve.wait_ge(rstd_done, {0: 2, 1: 3, 4: 8, 5: 9}[p])
                else:
                    mx = MIX_NO[p]
                    for c in range(4):
                        split_lo(b + RING, 0, c)
                    mean(nrm)

                    def qk_mean(u):
                        g = 8 * mx + u
                        dve.wait_ge(qst_mm, g + 1)
                        if g:
                            dve.wait_ge(qpow_done, g)
                        if u == 0:
                            dve.wait_ge(pow_done, nrm + 1)
                        nc.vector.tensor_scalar(var[:], bank[4][:, 0:8], 1.0 / HD, EPS, ALU.mult, ALU.add)\
                            .then_inc(qvar_done, 1)

                    def qk_scale(u):
                        g, t = 8 * mx + u, u // 2
                        dve.wait_ge(qr_done, g + 1)
                        if u % 2 == 0:
                            dst, gc = col(q_sb, t * T, T), qg[:, 0:1]
                        else:
                            dst, gc = col(k_sb, t * S + mx * T, T), sm[:, SM_KG:SM_KG + 1]
                        nc.vector.scalar_tensor_tensor(dst, bank[u % 4][:], gc, sq[:], ALU.mult, ALU.mult)\
                            .then_inc(qk_done, 1)

                    for u in range(8):
                        split_lo(b + RING + MIX_QK, 0, u)
                        if u >= 1:
                            qk_mean(u - 1)
                        if u >= 2:
                            qk_scale(u - 2)
                    for c in range(8):
                        ct = c % 4
                        if c < 2:
                            if c == 0:
                                qk_mean(7)
                            qk_scale(6 + c)
                        split_lo(b + RING + MIX_CONV, 0, c)
                        ug = col(u_sb, ct * UW, UW)
                        cgt = col(cg, ct * T, T)
                        cv = 4 * (KA * mx + ct)
                        if c >= 4:
                            if mx == 0:
                                nc.vector.memset(ug[:, 0:2], 0.0).then_inc(halo_done, 1)
                            else:
                                nc.vector.tensor_copy(ug[:, 0:2], halo[:, 2 * ct:2 * ct + 2]).then_inc(halo_done, 1)
                            dve.wait_ge(cg_done, KA * mx + ct + 1)
                            dve.wait_ge(w_used, b + MIX_CONV + c + 1)
                            nc.vector.tensor_tensor(ug[:, 2:UW], bank[ct][:], cgt, ALU.mult).then_inc(cv_chain, 1)
                            dve.wait_ge(halo_done, 2 * KA * mx + ct + 1)
                            dve.wait_ge(cv_chain, cv + 1)
                            nc.vector.tensor_scalar(cgt, ug[:, 2:UW], wc(2, ct), sm[:, SM_BC + ct:SM_BC + ct + 1],
                                                    ALU.mult, ALU.add).then_inc(cv_chain, 1)
                            for tap in (1, 0):
                                dve.wait_ge(cv_chain, cv + 3 - tap)
                                nc.vector.scalar_tensor_tensor(cgt, ug[:, tap:tap + T], wc(tap, ct), cgt,
                                                               ALU.mult, ALU.add).then_inc(cv_chain, 1)

                    def conv_gate(ct):
                        dve.wait_ge(w_used, b + MIX_CONV + 8 + ct + 1)
                        dve.wait_ge(cv_chain, 4 * (KA * mx + ct) + 4)
                        nc.vector.tensor_tensor(col(yc, ct * T, T), bank[GATE_B[ct]][:], col(cg, ct * T, T), ALU.mult)\
                            .then_inc(yc_done, 1)
                        if mx == 0:
                            nc.vector.tensor_copy(halo[:, 2 * ct:2 * ct + 2], u_sb[:, ct * UW + T:(ct + 1) * UW])\
                                .then_inc(halo_done, 1)

                    def conv_first(ct):
                        g = KA * mx + ct
                        dve.wait_ge(rstd_done, NORM_CONV[p] + 1) if ct == 0 else None
                        dve.wait_ge(yc_ready, g) if g else None
                        nc.vector.scalar_tensor_tensor(tmp[:], col(yc, ct * T, T), sm[:, SM_GC + ct:SM_GC + ct + 1],
                                                       col(rstd, (p % 2) * T, T), ALU.mult, ALU.mult).then_inc(y_tmp, 1)

                    def conv_second(ct):
                        dve.wait_ge(y_hi_done, KA * mx + ct + 1)
                        yl = (KA + ct) * T
                        nc.vector.tensor_tensor(col(y_lo, yl, T), tmp[:], col(y_hi, yl, T).bitcast(F32),
                                                ALU.subtract).then_inc(yc_ready, 1)

                    def scores(s):
                        qt, h = s // HEADS, s % HEADS
                        nb = key_tiles(mx, qt)
                        g = UNITS * mx + s
                        dve.wait_ge(s_mm, g + 1)
                        if g >= 2:
                            dve.wait_ge(t_mm, g - 1)
                        if qt == 0:
                            dve.wait_ge(bias_ok, 2 * (HEADS * mx + h + 1))
                        if s == 0:
                            dve.wait_ge(h_free, (KD - 1) * mx + H_EARLY)
                        off = (s % 2) * BANDW
                        nc.vector.tensor_tensor_reduce(
                            out=s_sb[:, off:off + nb * P], in0=spair(s)[:, 0:nb * P],
                            in1=bias[:, (h + 1) * BANDW - nb * P:(h + 1) * BANDW],
                            scale=-1.0, scalar=3e38, op0=ALU.add, op1=ALU.min,
                            accum_out=nmax[:, s % 2:s % 2 + 1]).then_inc(s_done, 1)

                    def probs(s):
                        qt = s // HEADS
                        nb = key_tiles(mx, qt)
                        g = UNITS * mx + s
                        dve.wait_ge(t_mm, g + 1)
                        if g >= 2:
                            dve.wait_ge(pv_mm, g - 1)
                        off = (s % 2) * BANDW
                        nc.vector.tensor_copy(pT[:, off:off + nb * P], tpair[:, 0:nb * P]).then_inc(pt_done, 1)

                    def y_rows(qt):
                        n = TT * mx + qt
                        dve.wait_ge(pv_mm, UNITS * mx + HEADS * (qt + 1))
                        r = (qt % 2) * HEADS
                        if n:
                            dve.wait_ge(yt_done, n)
                        nc.vector.reciprocal(rrec[:], rsum[:, r:r + HEADS]).then_inc(rrec_done, 1)
                        dve.wait_ge(rrec_done, n + 1)
                        if n:
                            dve.wait_ge(yT_mm, n)
                        rb = bass.AP(rrec[:].tensor, rrec[:].offset, [list(rrec[:].ap[0]), [1, HEADS], [0, HD]])
                        nc.vector.tensor_tensor(ytok[:].rearrange("p (h d) -> p h d", h=HEADS),
                                                y_bank(qt)[:].rearrange("p (h d) -> p h d", h=HEADS), rb,
                                                ALU.mult).then_inc(yt_done, 1)

                    def y_norm(qt):
                        n = TT * mx + qt
                        dve.wait_ge(ysq_done, n + 1)
                        if n:
                            dve.wait_ge(ypow_done, n)
                        nc.vector.tensor_scalar(yvar[:], ssum[:], 1.0 / DA, EPS, ALU.mult, ALU.add).then_inc(yvar_done, 1)

                    def y_norm2(qt):
                        n = TT * mx + qt
                        dve.wait_ge(ypow_done, n + 1)
                        dve.wait_ge(grow_in, 16)
                        nc.vector.scalar_tensor_tensor(ytok[:], ytok[:], yr[:, 0:1], g_row[:], ALU.mult, ALU.mult)\
                            .then_inc(yn_done, 1)

                    def y_low(qt):
                        n = TT * mx + qt
                        dve.wait_ge(ya_hi_done, n + 1)
                        yb = y_bank(qt)
                        src = bass.AP(yb[:].tensor, yb[:].offset + P - 1, [list(yb[:].ap[0]), [P, KA], [-1, P]])
                        c = tile_at(mx, qt) * P
                        sl = slice(c, c + P)
                        hi = y_hi[:, 0:KA * T].rearrange("p (t c) -> p t c", t=KA)[:, :, sl]
                        lo = y_lo[:, 0:KA * T].rearrange("p (t c) -> p t c", t=KA)[:, :, sl]
                        nc.vector.tensor_tensor(lo, src, hi.bitcast(F32), ALU.subtract).then_inc(ya_ready, 1)

                    for s in range(UNITS + 3):
                        if s < UNITS:
                            scores(s)
                        if s == 1:
                            for ct in range(KA):
                                conv_gate(ct)
                        if 2 <= s < UNITS + 2:
                            probs(s - 2)
                        if 0 <= s - CONV_SQUARE - 1 < KA:
                            add_square(NORM_CONV[p], s - CONV_SQUARE - 1)
                        if s == CONV_STATS:
                            mean(NORM_CONV[p])
                        if s - 1 in CONV_SPLIT[mx]:
                            conv_second(CONV_SPLIT[mx].index(s - 1))
                        if s in CONV_SPLIT[mx]:
                            conv_first(CONV_SPLIT[mx].index(s))
                        if s > HEADS:
                            qt = s // HEADS - 1
                            if s % HEADS == 3:
                                y_rows(qt)
                            if s % HEADS == 5 and s < UNITS:
                                y_norm(qt)
                            if s % HEADS == 6 and s < UNITS:
                                y_norm2(qt)
                            if s % HEADS == 0 and s > HEADS:
                                y_low(qt - 1)
                    y_rows(TT - 1)
                    y_norm(TT - 1)
                    y_norm2(TT - 1)
                    y_low(TT - 1)
                if kind == "ffn":
                    dve.wait_ge(hid_done, CREDIT + J_BASE[p] + KF)
                else:
                    dve.wait_ge(yc_ready, KA * (mx + 1))
                    dve.wait_ge(w_ready, b + nin + 4)
                if p + 1 < len(PHASES):
                    with dve.Fori(0, 2) as i:
                        for m in range(4):
                            out_tile(p, i, m, False)
                else:
                    for i in range(2):
                        for m in range(4):
                            out_tile(p, i, m, i == 1)
            mean(9)
            dve.wait_ge(rstd_done, 10)
            for m in range(KD):
                final(m, 1, out_sb1)

        @block.tensor
        def _(pe):
            def passes(dst, lh, ll, rh, rl, first, last):
                nc.tensor.matmul(dst, lh, rh, start=first, stop=False)
                nc.tensor.matmul(dst, lh, rl, start=False, stop=False)
                return nc.tensor.matmul(dst, ll, rh, start=False, stop=last)

            def w_block(slot, k):
                c = slot * CW + k * P
                return w_hi[:, c:c + P], w_lo[:, c:c + P]

            def act_tile(hi, lo, k):
                return hi[:, k * T:(k + 1) * T], lo[:, k * T:(k + 1) * T]

            def norm_stats(n):
                pe.wait_ge(acc_done, norm_acc(n) + 1 + NORM_TILES[n])
                for t in range(TT):
                    mm = nc.tensor.matmul(bank[STAT][:, t:t + 1], acc[:, t * P:(t + 1) * P], one2[:, 0:1],
                                          start=True, stop=True)
                mm.then_inc(stat_mm, 1)

            def norm_spread(n):
                pe.wait_ge(pow_done, n + 1)
                for t in range(TT):
                    r = rinv[:, t:t + 1]
                    src = bass.AP(r.tensor, r.offset, [list(r.ap[0]), [0, P]])
                    mm = nc.tensor.transpose(bank[STAT][:, t * P:(t + 1) * P], src, ident[:])
                mm.then_inc(bc_done, 1)

            def ada_column(f, src, k):
                return nc.tensor.matmul(bank[ADAB][:, bass.ds(f, 1)], src[:, k * P:(k + 1) * P], one2[:, 0:1],
                                        start=True, stop=True)

            def ada_summed(n, done):
                f, tiles = ADA_SUMS[n]
                pe.wait_ge(ada_chain, KD * (n + 1))
                for k in range(tiles):
                    if tiles == 3:
                        ada_column(f + k, ada_acc2, k + (0 if n == 1 else 3)).then_inc(done, 1)
                    else:
                        ada_column(f + k, ada_acc, k).then_inc(done, 1)

            def ada_direct(f):
                pe.wait_ge(ada0_in[f // ADA_GROUP], 16)
                for k in range(KD):
                    mm = nc.tensor.matmul(bank[ADAB][:, f:f + 1], ada0[:, f * CW + k * P:f * CW + (k + 1) * P],
                                          s_c[:, k:k + 1], start=(k == 0), stop=(k == KD - 1))
                mm.then_inc(ada_mm, 1)

            def hidden_ada(p, i, jj):
                if p in ADA_IN_BASE:
                    f = ADA_IN_BASE[p] + jj + 2 * i
                    pe.wait_ge(ada_ready, f - ADA_FIRST + 1)
                    ada_column(f, ada_w, 0).then_inc(ada_mm, 1)

            pe.wait_ge(const_done, 6)
            pe.wait_ge(sc_done, 1)
            norm_stats(0)
            norm_spread(0)
            ada_direct(11)
            ada_summed(0, ada_mm)
            ada_summed(1, ada_mm)

            def first_tiles(jj, k0, k1):
                for k in range(k0, k1):
                    pe.wait_ge(h_ready, k + 1)
                    for part in range(2):
                        c = 2 * jj + part
                        pe.wait_ge(w_ready, c + 1)
                        mm = passes(bank[2 * part + jj][:], *w_block(c, k), *act_tile(h_hi, h_lo, k), k == 0, k == KD - 1)
                        if k == KD - 1:
                            mm.then_inc(w_used, 1)

            first_tiles(0, 0, KD // 2)
            pe.wait_ge(mod_chain, 3)
            hidden_ada(0, 0, 0)
            ada_direct(15)
            ada_summed(2, ada_mm)
            ada_summed(3, ada_mm)
            first_tiles(1, 0, KD // 2)
            first_tiles(0, KD // 2, KD)
            pe.wait_ge(mod_chain, 6)
            hidden_ada(0, 0, 1)
            first_tiles(1, KD // 2, KD)

            def ffn_in(p, i, jj):
                b, j0 = CHUNK_BASE[p], J_BASE[p]
                for part in range(2):
                    c = 2 * jj + part
                    pe.wait_ge(w_ready, b + c + 1 + 4 * i)
                    pe.wait_ge(gate_done if part == 0 else prod_done, CREDIT - 1 + j0 + jj + 2 * i)
                    if part == 1 and jj == 1:
                        pe.wait_ge(x_done, CREDIT + KD * p)
                    dst = bank[2 * part + jj]
                    for k in range(KD):
                        mm = passes(dst[:], *w_block(c, k), *act_tile(h_hi, h_lo, k), k == 0, k == KD - 1)
                    mm.then_inc(w_used, 1)
                hidden_ada(p, i, jj)

            for p in range(len(PHASES)):
                b, nin, kind = ph(p)
                nrm = NORM_IN_PHASE[p]
                if p and kind == "ffn" and PHASES[p - 1] == "ffn":
                    pe.wait_ge(h_ready, KD * (p + 1))
                    pe.wait_ge(x_done, CREDIT + KD * p - 1)
                if kind == "ffn":
                    if p == 0:
                        for jj in range(2):
                            ffn_in(p, 1, jj)
                        ada_summed(4, ada_rest_mm)
                    if p == 4:
                        for k0 in (0, KD // 2):
                            for part in range(2):
                                pe.wait_ge(w_ready, b + part + 1)
                                pe.wait_ge(x_done, CREDIT + KD * p - 3 + 2 * part)
                                for k in range(k0, k0 + KD // 2):
                                    pe.wait_ge(h_ready, KD * p + k + 1)
                                    mm = passes(bank[2 * part][:], *w_block(part, k), *act_tile(h_hi, h_lo, k),
                                                k == 0, k == KD - 1)
                                if k == KD - 1:
                                    mm.then_inc(w_used, 1)
                        ffn_in(p, 0, 1)
                    with pe.Fori({0: 2, 4: 1}.get(p, 0), KF // 2 - 1) as i:
                        for jj in range(2):
                            ffn_in(p, i, jj)
                    norm_stats(nrm)
                    for jj in range(2):
                        ffn_in(p, KF // 2 - 1, jj)
                    norm_spread(nrm)
                    pe.wait_ge(gate_done, CREDIT + J_BASE[p] + KF - 1)

                    def out_col(p, i, m):
                        n = b + nin + 3 * m
                        k = 0
                        for c, nb in enumerate(OUT_BLOCKS):
                            pe.wait_ge(w_ready, n + c + 1 + 12 * i)
                            pe.wait_ge(hid_done, CREDIT + J_BASE[p] + (16 if c < 2 else KF))
                            if c == 0:
                                pe.wait_ge(x_done, CREDIT + KD * p + m - 3 + 4 * i)
                            for e in range(nb):
                                mm = passes(bank[m][:], *w_block((3 * m + c) % RING, e), *act_tile(hid_hi, hid_lo, k),
                                            k == 0, k == KF - 1)
                                k += 1
                            mm.then_inc(w_used, 1)
                        if p in ADA_OUT_BASE:
                            f = ADA_OUT_BASE[p] + m + 4 * i
                            pe.wait_ge(mod_chain, 11)
                            pe.wait_ge(ada_ready, f - ADA_FIRST + 1)
                            ada_column(f, ada_w, 0).then_inc(ada_mm, 1)
                    with pe.Fori(0, 2) as i:
                        for m in range(4):
                            out_col(p, i, m)
                else:
                    mx = MIX_NO[p]
                    for c in range(4):
                        pe.wait_ge(w_ready, b + c + 1)
                        for kk in range(2):
                            k = 2 * c + kk
                            pe.wait_ge(h_ready, KD * p + k + 1)
                            wh = w_hi[:, c * CW + kk * DA:c * CW + (kk + 1) * DA]
                            wl = w_lo[:, c * CW + kk * DA:c * CW + (kk + 1) * DA]
                            for t in range(TT):
                                a = k * T + t * P
                                mm = passes(bank[4 + t][:], h_hi[:, a:a + P], h_lo[:, a:a + P], wh, wl, k == 0, k == KD - 1)
                        mm.then_inc(w_used, 1)

                    def projection(n, bk):
                        pe.wait_ge(w_ready, n + 1)
                        for k in range(KD):
                            mm = passes(bank[bk][:], *w_block(n % RING, k), *act_tile(h_hi, h_lo, k), k == 0, k == KD - 1)
                        mm.then_inc(w_used, 1)

                    def qk_stats(u):
                        g = 8 * mx + u
                        pe.wait_ge(qsq_done, g + 1)
                        pe.wait_ge(qvar_done, g) if g else None
                        pe.wait_ge(v_done, TT * (mx + 1)) if u == 0 else None
                        for t in range(TT):
                            mm = nc.tensor.matmul(bank[4][:, 2 * t:2 * t + 2], qsq[:, t * P:(t + 1) * P], one2[:, 1:3],
                                                  start=True, stop=True)
                        mm.then_inc(qst_mm, 1)

                    def qk_spread(u):
                        g = 8 * mx + u
                        pe.wait_ge(qrow_done, g + 1)
                        pe.wait_ge(qr_done, g) if g else None
                        for t in range(TT):
                            mm = nc.tensor.transpose(bank[5][:, t * P:(t + 1) * P], qrow[:, t * P:(t + 1) * P], ident[:])
                        mm.then_inc(qbc_done, 1)

                    pe.wait_ge(x_done, CREDIT + KD * p)
                    for u in range(8):
                        if u >= 4:
                            pe.wait_ge(qk_done, 8 * mx + u - 3)
                        projection(b + MIX_QK + u, u % 4)
                        if u == 0:
                            pe.wait_ge(v_done, TT * (mx + 1))
                            norm_stats(nrm)
                        if u == 1:
                            norm_spread(nrm)
                        if u >= 1:
                            qk_stats(u - 1)
                        if u >= 2:
                            qk_spread(u - 2)
                    for c in range(8):
                        if c < 4:
                            pe.wait_ge(qk_done, 8 * mx + 5 + c)
                        else:
                            pe.wait_ge(cg_done, KA * mx + c - 3)
                        projection(b + MIX_CONV + c, c % 4)
                        if c == 0:
                            qk_stats(7)
                            qk_spread(6)
                        if c == 1:
                            qk_spread(7)
                    def score_mm(s):
                        qt, h = s // HEADS, s % HEADS
                        g = UNITS * mx + s
                        qg_ = TT * mx + qt
                        nb = key_tiles(mx, qt)
                        keys_end = TT * mx + tile_at(mx, qt) + 1
                        r0 = (h % 2) * HD
                        if h == 0:
                            pe.wait_ge(qrev_done, qg_ + 1)
                        if s >= 2:
                            pe.wait_ge(s_done, g - 1)
                        elif s == 0:
                            pe.wait_ge(cv_chain, 4 * (KA * mx + KA - 1) + 1)
                        lhs = q_rev[qt % 2][r0:r0 + HD, (h // 2) * P:(h // 2 + 1) * P]
                        c0 = (h // 2) * S + (keys_end - nb) * P
                        for a in range(0, nb * P, 512):
                            w = min(512, nb * P - a)
                            mm = nc.tensor.matmul(spair(s)[:, a:a + w], lhs, k_sb[r0:r0 + HD, c0 + a:c0 + a + w],
                                                  start=True, stop=True)
                        mm.then_inc(s_mm, 1)

                    def prob_mm(s):
                        qt = s // HEADS
                        g = UNITS * mx + s
                        nb = key_tiles(mx, qt)
                        pe.wait_ge(p_done, g + 1)
                        pe.wait_ge(pt_done, g) if g else None
                        pe.wait_ge(yc_done, KA * (mx + 1)) if s == 0 else None
                        for a in range(nb):
                            off = (s % 2) * BANDW + a * P
                            mm = nc.tensor.transpose(tpair[:, a * P:(a + 1) * P], s_sb[:, off:off + P], ident[:])
                        mm.then_inc(t_mm, 1)

                    def value_mm(s):
                        qt, h = s // HEADS, s % HEADS
                        qg_ = TT * mx + qt
                        g = UNITS * mx + s
                        nb = key_tiles(mx, qt)
                        keys_end = TT * mx + tile_at(mx, qt) + 1
                        pe.wait_ge(pt_done, g + 1)
                        if h == 0 and qt >= 2:
                            pe.wait_ge(ya_ready, qg_ - 1)
                        if h == 0 and qt == 1:
                            pe.wait_ge(rstd_done, NORM_CONV[p] + 1)
                        for a in range(nb):
                            off = (s % 2) * BANDW + a * P
                            kt = keys_end - nb + a
                            mm = nc.tensor.matmul(y_bank(qt)[:, h * HD:(h + 1) * HD], pT[:, off:off + P],
                                                  v_sb[:, kt * DA + h * HD:kt * DA + (h + 1) * HD],
                                                  start=(a == 0), stop=(a == nb - 1))
                        mm.then_inc(pv_mm, 1)

                    def y_turn(qt):
                        n = TT * mx + qt
                        pe.wait_ge(yn_done, n + 1)
                        for t in range(KA):
                            mm = nc.tensor.transpose(y_bank(qt)[:, t * P:(t + 1) * P], ytok[:, t * P:(t + 1) * P], ident[:])
                        mm.then_inc(yT_mm, 1)

                    pe.wait_ge(qvar_done, 8 * (mx + 1))
                    pe.wait_ge(qr_done, 8 * (mx + 1))
                    pe.wait_ge(rstd_done, nrm + 1)
                    for k in range(KD):
                        if k == H_EARLY:
                            score_mm(0)
                            score_mm(1)
                        for ct in range(KA):
                            n = b + MIX_CONV + 8 + ct
                            pe.wait_ge(w_ready, n + 1)
                            mm = passes(bank[GATE_B[ct]][:], *w_block(n % RING, k), *act_tile(h_hi, h_lo, k),
                                        k == 0, k == KD - 1)
                            if k == KD - 1:
                                mm.then_inc(w_used, 1)
                        if k < KD - 1:
                            mm.then_inc(h_free, 1)

                    def out_part(i, m, part):
                        pe.wait_ge(w_ready, b + nin + m + 1 + 4 * i)
                        pe.wait_ge(x_done, CREDIT + KD * p + m - 3 + 4 * i)
                        pe.wait_ge(yc_ready, KA * (mx + 1)) if part == 0 else pe.wait_ge(ya_ready, TT * (mx + 1))
                        for e in range(KA):
                            k = (KA, 0)[part] + e
                            mm = passes(bank[m][:], *w_block(m, k), *act_tile(y_hi, y_lo, k),
                                        part == 0 and e == 0, part == 1 and e == KA - 1)
                        if part == 1:
                            mm.then_inc(w_used, 1)

                    for s in range(2, UNITS + 3):
                        if s < UNITS:
                            score_mm(s)
                        if 2 <= s < UNITS + 2:
                            prob_mm(s - 2)
                        if s >= 3:
                            value_mm(s - 3)
                        if mx == 0 and s in OUT_EARLY:
                            out_part(0, OUT_EARLY[s], 0)
                        if s == CONV_STATS:
                            norm_stats(NORM_CONV[p])
                        if s == CONV_SPREAD:
                            norm_spread(NORM_CONV[p])
                        if s % HEADS == 7 and HEADS < s < UNITS:
                            y_turn(s // HEADS - 1)

                    out_part(0, 0, 0)
                    out_part(0, 2 if mx == 0 else 1, 0)
                    y_turn(TT - 1)
                    if mx == 1:
                        out_part(0, 2, 0)
                    for m in range(3):
                        out_part(0, m, 1)
                    if mx == 1:
                        out_part(0, 3, 0)
                    out_part(0, 3, 1)
                    for m in range(4):
                        for part in range(2):
                            out_part(1, m, part)
            norm_stats(9)
            norm_spread(9)


def kernel(**inputs):
    import numpy as np
    import concourse.bacc as bacc
    from concourse import mybir as mb
    from concourse.bass_utils import run_bass_kernel_spmd
    g = {k: np.asarray(v) for k, v in inputs.items()}

    def blocks(w):
        k, m = w.shape[0] // P, w.shape[1] // P
        return w.reshape(k, P, m, P).transpose(2, 1, 0, 3).reshape(m, P, k * P)

    def ffn_in(w):
        b = blocks(w)
        return b.reshape(2, KF, P, CW).transpose(1, 0, 2, 3).reshape(2 * KF, P, CW)

    w_in = g["w_in"][0]
    tiles = blocks(w_in)
    v = w_in[:, 2 * DA:3 * DA].reshape(4, 2, P, DA).transpose(0, 2, 1, 3).reshape(4, P, CW)
    order = [t for k in range(KA) for t in (k, KA + k)]
    order += [5 * KA + k for k in range(KA)] + [3 * KA + k for k in range(KA)] + [4 * KA + k for k in range(KA)]
    cols = lambda a: a.reshape(-1, P).T
    two = lambda a: np.concatenate([a.reshape(-1), a.reshape(-1)]).reshape(P, 1)
    arrays = {
        "xT": g["x"][0].reshape(HALVES, T, KD, P).transpose(0, 3, 2, 1).reshape(HALVES, P, KD * T),
        "w_ada": blocks(g["w_ada"][0]),
        "small": np.concatenate([cols(g["c"][0]), cols(g["b_ada"][0]), cols(g["g_norm"][0]), cols(g["g_final"][0]),
                                 two(g["q_norm_g"][0]), two(g["k_norm_g"][0]), cols(g["w_conv"][0]),
                                 cols(g["b_conv"][0]), cols(g["g_conv_out"][0])], axis=1),
        "w_f1i": ffn_in(g["w_ffn1_in"][0]), "w_f1o": blocks(g["w_ffn1_out"][0]),
        "w_mix": np.concatenate([v, tiles[order]]), "w_mo": blocks(g["w_out"][0]),
        "w_f2i": ffn_in(g["w_ffn2_in"][0]), "w_f2o": blocks(g["w_ffn2_out"][0]),
        "bias_ext": np.pad(g["rel_bias"][0][:, :2 * MAX_REL], ((0, 0), (BANDW + P - 1 - 2 * MAX_REL, 0)), mode="edge"),
        "g_attn": g["g_attn_out"][0],
    }
    nc = bacc.Bacc("TRN2", target_bir_lowering=False, num_devices=1)
    feed, args = {}, []
    for name, a in arrays.items():
        feed[name] = np.ascontiguousarray(a)
        args.append(nc.dram_tensor(name, a.shape, mb.dt.from_np(a.dtype), kind="ExternalInput").ap())
    args.append(nc.dram_tensor("out", (HALVES * KD, P, T), mb.dt.float32, kind="ExternalOutput").ap())
    build(nc, *args)
    r = run_bass_kernel_spmd(nc, [feed], core_ids=[0]).results[0]["out"]
    y = np.asarray(r).reshape(HALVES, KD, P, T).transpose(0, 3, 1, 2).reshape(1, S, D)
    return np.ascontiguousarray(y)
```
